# Optimizing a Trainium2 kernel written in Bass

```python
import math
import jax, jax.numpy as jnp
from jax import lax
import numpy as np

D_MODEL = 1024
BATCH = 1
SEQ = 512
DEPTH = 2
DEC_BATCH = 8
DEC_SEQ = 1
PAST_LEN = 1024
PAGE_SIZE = 128

N_MIXERS = 2
N_SWA_LAYERS = (DEPTH + 1) // 2
N_SSM_LAYERS = DEPTH // 2
HEAD_DIM = 64
N_HEADS = D_MODEL // HEAD_DIM
N_KV_HEADS = 4
GQA_GROUP = N_HEADS // N_KV_HEADS
WINDOW = 128
ATTN_BLOCK = WINDOW
CACHE_WIN = min(WINDOW, PAST_LEN)
PROMPT_WIN = min(WINDOW, SEQ)
SSM_GROUP = 16
N_SSM_GROUPS = D_MODEL // SSM_GROUP
SSM_STATE = 64
D_FF = 2816
CONV_W = 3
RMS_EPS = 1e-6
DT_MIN = 1e-3
DT_MAX = 1e-1

kernel_name = "swa_sink_s5_convffn_hybrid_step"

F32 = jnp.float32

def rmsnorm(x, g):
    xf = x.astype(F32)
    y = xf * lax.rsqrt(jnp.mean(xf * xf, axis=-1, keepdims=True) + RMS_EPS)
    return (y * g.astype(F32)).astype(x.dtype)

def qkv_project(h, w_qkv, q_gain, k_gain):
    n, l, _ = h.shape
    qkv = h @ w_qkv
    q, k, v = jnp.split(qkv, [N_HEADS * HEAD_DIM, (N_HEADS + N_KV_HEADS) * HEAD_DIM], axis=-1)
    q = rmsnorm(q.reshape(n, l, N_KV_HEADS, GQA_GROUP, HEAD_DIM), q_gain)
    k = rmsnorm(k.reshape(n, l, N_KV_HEADS, HEAD_DIM), k_gain)
    v = v.reshape(n, l, N_KV_HEADS, HEAD_DIM)
    return q, k, v

def sink_attend(scores, valid, sink, v, eq):
    scores = jnp.where(valid, scores, -jnp.inf)
    sink_col = jnp.broadcast_to(sink.astype(F32).reshape(N_KV_HEADS, GQA_GROUP, 1, 1),
                                scores.shape[:-1] + (1,))
    probs = jax.nn.softmax(jnp.concatenate([scores, sink_col], axis=-1), axis=-1)[..., :-1]
    return jnp.einsum(eq, probs.astype(v.dtype), v)

def swa_prompt(h, w_qkv, w_o, q_gain, k_gain, sink):
    n, l, _ = h.shape
    nb = l // ATTN_BLOCK
    q, k, v = qkv_project(h, w_qkv, q_gain, k_gain)
    qb = q.reshape(n, nb, ATTN_BLOCK, N_KV_HEADS, GQA_GROUP, HEAD_DIM)
    kb = k.reshape(n, nb, ATTN_BLOCK, N_KV_HEADS, HEAD_DIM)
    vb = v.reshape(n, nb, ATTN_BLOCK, N_KV_HEADS, HEAD_DIM)

    def band(t):
        prev = jnp.concatenate([jnp.zeros_like(t[:, :1]), t[:, :-1]], axis=1)
        return jnp.concatenate([prev, t], axis=2)

    kk, vv = band(kb), band(vb)
    scores = jnp.einsum('nbqkgd,nbskd->nbkgqs', qb.astype(F32), kk.astype(F32)) * HEAD_DIM ** -0.5
    blk = jnp.arange(nb)[:, None, None]
    qpos = blk * ATTN_BLOCK + jnp.arange(ATTN_BLOCK)[None, :, None]
    kpos = (blk - 1) * ATTN_BLOCK + jnp.arange(2 * ATTN_BLOCK)[None, None, :]
    diff = qpos - kpos
    valid = (diff >= 0) & (diff < WINDOW) & (kpos >= 0)
    o = sink_attend(scores, valid[:, None, None], sink, vv, 'nbkgqs,nbskd->nbqkgd')
    o = o.reshape(n, l, N_HEADS * HEAD_DIM) @ w_o
    return o, k[:, -PROMPT_WIN:], v[:, -PROMPT_WIN:]

def swa_sample(h, cache_k, cache_v, w_qkv, w_o, q_gain, k_gain, sink):
    n, s, _ = h.shape
    q, k, v = qkv_project(h, w_qkv, q_gain, k_gain)
    kk = jnp.concatenate([cache_k.astype(k.dtype), k], axis=1)
    vv = jnp.concatenate([cache_v.astype(v.dtype), v], axis=1)
    scores = jnp.einsum('nqkgd,nskd->nkgqs', q.astype(F32), kk.astype(F32)) * HEAD_DIM ** -0.5
    qpos = PAST_LEN + jnp.arange(s)[:, None]
    kpos = jnp.concatenate([PAST_LEN - CACHE_WIN + jnp.arange(CACHE_WIN),
                            PAST_LEN + jnp.arange(s)])[None, :]
    diff = qpos - kpos
    valid = (diff >= 0) & (diff < WINDOW)
    o = sink_attend(scores, valid, sink, vv, 'nkgqs,nskd->nqkgd')
    o = o.reshape(n, s, N_HEADS * HEAD_DIM) @ w_o
    return o, kk[:, -CACHE_WIN:], vv[:, -CACHE_WIN:]

def s5_discretize(a_re, a_im, log_dt, b_re, b_im):
    a_re, a_im = a_re.astype(F32), a_im.astype(F32)
    dt = jnp.exp(log_dt.astype(F32))[:, None]
    mag = jnp.exp(a_re * dt)
    ab_re, ab_im = mag * jnp.cos(a_im * dt), mag * jnp.sin(a_im * dt)
    den = a_re * a_re + a_im * a_im
    c_re = ((ab_re - 1.0) * a_re + ab_im * a_im) / den
    c_im = (ab_im * a_re - (ab_re - 1.0) * a_im) / den
    b_re, b_im = b_re.astype(F32), b_im.astype(F32)
    bb_re = c_re[..., None] * b_re - c_im[..., None] * b_im
    bb_im = c_re[..., None] * b_im + c_im[..., None] * b_re
    return ab_re, ab_im, bb_re, bb_im

def complex_affine_combine(e1, e2):
    a1r, a1i, b1r, b1i = e1
    a2r, a2i, b2r, b2i = e2
    return (a2r * a1r - a2i * a1i, a2r * a1i + a2i * a1r,
            a2r * b1r - a2i * b1i + b2r, a2r * b1i + a2i * b1r + b2i)

def s5_mixer(h, st_re, st_im, a_re, a_im, log_dt, b_re, b_im, c_re, c_im, d_skip, w_glu):
    n, l, _ = h.shape
    ab_re, ab_im, bb_re, bb_im = s5_discretize(a_re, a_im, log_dt, b_re, b_im)
    u = h.astype(F32).reshape(n, l, N_SSM_GROUPS, SSM_GROUP)
    bu_re = jnp.einsum('nlgc,gpc->nlgp', u, bb_re)
    bu_im = jnp.einsum('nlgc,gpc->nlgp', u, bb_im)
    h0_re, h0_im = st_re.astype(F32), st_im.astype(F32)
    bu_re = bu_re.at[:, 0].add(ab_re * h0_re - ab_im * h0_im)
    bu_im = bu_im.at[:, 0].add(ab_re * h0_im + ab_im * h0_re)
    a_r = jnp.broadcast_to(ab_re, bu_re.shape)
    a_i = jnp.broadcast_to(ab_im, bu_im.shape)
    _, _, xr, xi = lax.associative_scan(complex_affine_combine, (a_r, a_i, bu_re, bu_im), axis=1)
    y = (jnp.einsum('nlgp,gcp->nlgc', xr, c_re.astype(F32))
         - jnp.einsum('nlgp,gcp->nlgc', xi, c_im.astype(F32)))
    y = y.reshape(n, l, D_MODEL) + d_skip.astype(F32) * h.astype(F32)
    z = jax.nn.gelu(y).astype(h.dtype)
    zz = z @ w_glu
    out = zz[..., :D_MODEL] * jax.nn.sigmoid(zz[..., D_MODEL:])
    return out, xr[:, -1].astype(st_re.dtype), xi[:, -1].astype(st_im.dtype)

def conv_ffn(h, buf, w_up, conv_w, conv_b, w_down):
    up = h @ w_up
    l = up.shape[1]
    padded = jnp.concatenate([buf.astype(up.dtype), up], axis=1)
    c = conv_b
    for j in range(CONV_W):
        c = c + conv_w[j] * padded[:, j:j + l]
    g, v = jnp.split(c, 2, axis=-1)
    out = (jax.nn.silu(g) * v) @ w_down
    return out, padded[:, -(CONV_W - 1):]

def trunk(x, cache_k, cache_v, st_re, st_im, st_conv, norm_mix, norm_ffn, w_qkv, w_o, q_norm,
          k_norm, sinks, ssm_a_re, ssm_a_im, ssm_log_dt, ssm_b_re, ssm_b_im, ssm_c_re, ssm_c_im,
          ssm_d, w_glu, w_up, conv_w, conv_b, w_down):
    ks, vs, srs, sis, cbs = [], [], [], [], []
    for i in range(DEPTH):
        j = i // N_MIXERS
        h = rmsnorm(x, norm_mix[i])
        if i % N_MIXERS == 0:
            if cache_k is None:
                o, nk, nv = swa_prompt(h, w_qkv[j], w_o[j], q_norm[j], k_norm[j], sinks[j])
            else:
                o, nk, nv = swa_sample(h, cache_k[j], cache_v[j], w_qkv[j], w_o[j], q_norm[j],
                                       k_norm[j], sinks[j])
            ks.append(nk)
            vs.append(nv)
        else:
            o, sr, si = s5_mixer(h, st_re[j], st_im[j], ssm_a_re[j], ssm_a_im[j], ssm_log_dt[j],
                                 ssm_b_re[j], ssm_b_im[j], ssm_c_re[j], ssm_c_im[j], ssm_d[j], w_glu[j])
            srs.append(sr)
            sis.append(si)
        x = x + o
        h = rmsnorm(x, norm_ffn[i])
        o, cb = conv_ffn(h, st_conv[i], w_up[i], conv_w[i], conv_b[i], w_down[i])
        cbs.append(cb)
        x = x + o
    return x, jnp.stack(ks), jnp.stack(vs), jnp.stack(srs), jnp.stack(sis), jnp.stack(cbs)

def setup_inputs(seed: int = 0) -> dict:
    key = jax.random.key(seed)
    k = jax.random.split(key, 32)
    nrm = jax.random.normal
    F2 = 2 * D_FF
    n_idx = jnp.arange(SSM_STATE, dtype=F32)
    return {
        "x_prompt": nrm(k[0], (BATCH, SEQ, D_MODEL), F32),
        "x_sample": nrm(k[1], (DEC_BATCH, DEC_SEQ, D_MODEL), F32),
        "cache_k": nrm(k[2], (N_SWA_LAYERS, DEC_BATCH, CACHE_WIN, N_KV_HEADS, HEAD_DIM), F32),
        "cache_v": nrm(k[3], (N_SWA_LAYERS, DEC_BATCH, CACHE_WIN, N_KV_HEADS, HEAD_DIM), F32),
        "state_ssm_re": 0.5 * nrm(k[4], (N_SSM_LAYERS, DEC_BATCH, N_SSM_GROUPS, SSM_STATE), F32),
        "state_ssm_im": 0.5 * nrm(k[5], (N_SSM_LAYERS, DEC_BATCH, N_SSM_GROUPS, SSM_STATE), F32),
        "state_conv": nrm(k[6], (DEPTH, DEC_BATCH, CONV_W - 1, F2), F32),
        "norm_mix": 1.0 + 0.05 * nrm(k[7], (DEPTH, D_MODEL), F32),
        "norm_ffn": 1.0 + 0.05 * nrm(k[8], (DEPTH, D_MODEL), F32),
        "w_qkv": nrm(k[9], (N_SWA_LAYERS, D_MODEL, (N_HEADS + 2 * N_KV_HEADS) * HEAD_DIM), F32) * D_MODEL ** -0.5,
        "w_o": nrm(k[10], (N_SWA_LAYERS, N_HEADS * HEAD_DIM, D_MODEL), F32) * (N_HEADS * HEAD_DIM) ** -0.5,
        "q_norm": 1.0 + 0.05 * nrm(k[11], (N_SWA_LAYERS, HEAD_DIM), F32),
        "k_norm": 1.0 + 0.05 * nrm(k[12], (N_SWA_LAYERS, HEAD_DIM), F32),
        "sinks": 0.5 * nrm(k[13], (N_SWA_LAYERS, N_HEADS), F32),
        "ssm_a_re": -0.5 + 0.01 * nrm(k[14], (N_SSM_LAYERS, N_SSM_GROUPS, SSM_STATE), F32),
        "ssm_a_im": math.pi * n_idx + 0.01 * nrm(k[15], (N_SSM_LAYERS, N_SSM_GROUPS, SSM_STATE), F32),
        "ssm_log_dt": jax.random.uniform(k[16], (N_SSM_LAYERS, N_SSM_GROUPS), F32,
                                         math.log(DT_MIN), math.log(DT_MAX)),
        "ssm_b_re": nrm(k[17], (N_SSM_LAYERS, N_SSM_GROUPS, SSM_STATE, SSM_GROUP), F32) * (2 * SSM_GROUP) ** -0.5,
        "ssm_b_im": nrm(k[18], (N_SSM_LAYERS, N_SSM_GROUPS, SSM_STATE, SSM_GROUP), F32) * (2 * SSM_GROUP) ** -0.5,
        "ssm_c_re": nrm(k[19], (N_SSM_LAYERS, N_SSM_GROUPS, SSM_GROUP, SSM_STATE), F32) * SSM_STATE ** -0.5,
        "ssm_c_im": nrm(k[20], (N_SSM_LAYERS, N_SSM_GROUPS, SSM_GROUP, SSM_STATE), F32) * SSM_STATE ** -0.5,
        "ssm_d": nrm(k[21], (N_SSM_LAYERS, D_MODEL), F32),
        "w_glu": nrm(k[22], (N_SSM_LAYERS, D_MODEL, 2 * D_MODEL), F32) * D_MODEL ** -0.5,
        "w_up": nrm(k[23], (DEPTH, D_MODEL, F2), F32) * D_MODEL ** -0.5,
        "conv_w": nrm(k[24], (DEPTH, CONV_W, F2), F32) * CONV_W ** -0.5,
        "conv_b": 0.01 * nrm(k[25], (DEPTH, F2), F32),
        "w_down": nrm(k[26], (DEPTH, D_FF, D_MODEL), F32) * D_FF ** -0.5,
    }

def reference(x_prompt, x_sample, cache_k, cache_v, state_ssm_re, state_ssm_im, state_conv,
              norm_mix, norm_ffn, w_qkv, w_o, q_norm, k_norm, sinks, ssm_a_re, ssm_a_im,
              ssm_log_dt, ssm_b_re, ssm_b_im, ssm_c_re, ssm_c_im, ssm_d, w_glu, w_up, conv_w,
              conv_b, w_down):
    dt = x_prompt.dtype
    zero_re = jnp.zeros((N_SSM_LAYERS, BATCH, N_SSM_GROUPS, SSM_STATE), dt)
    zero_im = jnp.zeros((N_SSM_LAYERS, BATCH, N_SSM_GROUPS, SSM_STATE), dt)
    zero_conv = jnp.zeros((DEPTH, BATCH, CONV_W - 1, 2 * D_FF), dt)
    y_prompt, k_prompt, v_prompt, ssm_re_prompt, ssm_im_prompt, conv_prompt = trunk(
        x_prompt, None, None, zero_re, zero_im, zero_conv, norm_mix, norm_ffn, w_qkv, w_o,
        q_norm, k_norm, sinks, ssm_a_re, ssm_a_im, ssm_log_dt, ssm_b_re, ssm_b_im, ssm_c_re,
        ssm_c_im, ssm_d, w_glu, w_up, conv_w, conv_b, w_down)
    y_sample, k_sample, v_sample, ssm_re_sample, ssm_im_sample, conv_sample = trunk(
        x_sample, cache_k, cache_v, state_ssm_re, state_ssm_im, state_conv, norm_mix, norm_ffn,
        w_qkv, w_o, q_norm, k_norm, sinks, ssm_a_re, ssm_a_im, ssm_log_dt, ssm_b_re, ssm_b_im,
        ssm_c_re, ssm_c_im, ssm_d, w_glu, w_up, conv_w, conv_b, w_down)
    return (y_prompt, y_sample, k_prompt, v_prompt, k_sample, v_sample, ssm_re_prompt,
            ssm_im_prompt, ssm_re_sample, ssm_im_sample, conv_prompt, conv_sample)


_drawn_inputs = setup_inputs


def setup_inputs(seed=0):
    import zlib

    import numpy as np

    out = dict(_drawn_inputs(seed))
    spreads = {}
    factors = {'q_norm': 5.752, 'sinks': 7.798, 'ssm_a_re': 4.093, 'conv_b': 5.534}
    for name, (base, spread) in spreads.items():
        noise = np.random.default_rng([zlib.crc32(name.encode()), seed]).standard_normal(out[name].shape)
        drawn = base * np.exp(spread * noise) if base else spread * noise
        out[name] = __import__('jax').numpy.asarray(drawn.astype(out[name].dtype))
    for name, factor in factors.items():
        out[name] = (out[name] * factor).astype(out[name].dtype)
    return out
```

```python
import math
from contextlib import ExitStack

import concourse.bass as bass
from concourse import mybir

ALU = mybir.AluOpType
ACT = mybir.ActivationFunctionType
AX = mybir.AxisListType
F32 = mybir.dt.float32
F32R = mybir.dt.float32r
BF16 = mybir.dt.bfloat16

P = 128
D, SEQ, NS = 1024, 512, 8
TOK = SEQ + NS
HALF = TOK // 2
KT = D // P
FF, F2 = 2816, 5632
NPAIR = FF // P // 2
HEADS, HD, KVH = 16, 64, 4
NB = SEQ // P
GROUPS, GC, ST = 64, 16, 64
CH = 8
NC = SEQ // CH
GP = GROUPS // 2
JQ = 4
NJ = GP // JQ
EPS = 1e-6
SCALE = HD ** -0.5
UCOL = 2 + TOK
MAGIC = 12582912.0
PI = math.pi

STAGES = [("qkv", "wqkv", 0, 12, KT), ("wo", "wo", 0, 8, KT)]
for _l in range(2):
    if _l:
        STAGES.append(("glu", "wglu", 0, 16, KT))
    for _h in range(2):
        STAGES.append((f"up{_l}{_h}", "wup", (_l * 2 + _h) * 2 * NPAIR, 2 * NPAIR, KT))
        STAGES.append((f"dn{_l}{_h}", "wdn", (_l * 2 + _h) * KT, KT, NPAIR))
BASE, _u = {}, 0
for _s in STAGES:
    BASE[_s[0]] = _u
    _u += _s[3]
ORDER = [s[0] for s in STAGES]
INFO = {s[0]: s for s in STAGES}
NORM_OF = {"qkv": 0, "up00": 1, "up10": 3}
PREPARES = {"wo": 1, "dn01": 2, "glu": 3}
HX_NORM = {0: 0, 1: 1, 3: 2}




def a_split(a):
    return a // 8, (a // 2) % 4, a % 2


def a_head(a):
    p, g, e = a_split(a)
    return 8 * p + 4 * e + g


def trunk_program(nc, i, o):
    with ExitStack() as ctx:
        sems = {}

        def sem(name):
            if name not in sems:
                sems[name] = ctx.enter_context(nc.semaphore(name))
            return sems[name]

        cur = [(nc.sbuf_base + 63) // 64 * 64]

        def place(name, cols, dt=F32, at=None):
            size = (cols * (2 if dt == BF16 else 4) + 31) // 32 * 32
            off = cur[0] if at is None else at
            if at is None:
                cur[0] += size
            t = nc.alloc_sbuf_tensor_at(name, [P, cols], dt, offset=off)
            return t, off

        x, _ = place("x", KT * TOK)
        w_raw, w_hi, w_lo = [], [], []
        for b in range(2):
            w_raw.append(place(f"w_raw{b}", NPAIR * P)[0])
            w_hi.append(place(f"w_hi{b}", NPAIR * P, F32R)[0])
            w_lo.append(place(f"w_lo{b}", NPAIR * P, F32R)[0])
        hx_hi, HX = place("hx_hi", KT * TOK, F32R)
        hx_lo, _ = place("hx_lo", KT * TOK, F32R)
        hid_hi, D0 = place("hid_hi", NPAIR * TOK, F32R)
        hid_lo, _ = place("hid_lo", NPAIR * TOK, F32R)
        op_hi, _ = place("op_hi", KT * TOK, F32R, at=D0)
        op_lo, _ = place("op_lo", KT * TOK, F32R, at=D0 + 4 * KT * TOK)
        D1 = cur[0]
        XW = NC + NS + 1
        UW = NC + 2 * NS
        cur[0] += 4 * (GROUPS * UW + 2 * GP * XW)
        qkvT, _ = place("qkvT", 12 * TOK, at=D1)
        vtok, _ = place("vtok", NB * 256, at=D1 + 48 * TOK)
        vc, _ = place("vc", NS * 256, at=D1 + 48 * TOK + 4096)
        kc, _ = place("kc", NS * 256, at=D0 + 8 * KT * TOK)
        new_rows, _ = place("new_rows", 512, at=D0 + 8 * KT * TOK + 8192)
        probs = [place(f"probs{b}", NB * 256, at=HX + 4096 * b)[0] for b in range(2)]
        probsT = [place(f"probsT{b}", 7 * P, at=HX + 8192 + 3584 * b)[0] for b in range(2)]
        ksT, _ = place("ksT", NS * 2 * P, at=HX + 15360)
        s_st, _ = place("s_st", P, at=HX + 23552)
        s_pr, _ = place("s_pr", P, at=HX + 24064)
        s_pT, _ = place("s_pT", P, at=HX + 24576)
        qk_rms = [place(f"qk_rms{b}", TOK, at=HX + 25088 + 2112 * b)[0] for b in range(2)]
        up_row = [place(f"up_row{b}", UCOL, at=D1 + 2112 * b)[0] for b in range(2)]
        conv = [place(f"conv{b}", TOK, at=D1 + 4224 + 2112 * b)[0] for b in range(2)]
        silu_g, _ = place("silu_g", TOK, at=D1 + 8448)
        hid, _ = place("hid", TOK, at=D1 + 10560)
        toep, _ = place("toep", CH * GROUPS * GC, at=D0)
        recs = [place(f"recs{b}", JQ * 2 * P, at=D0 + 32768 + 4096 * b)[0] for b in range(2)]
        rots = [place(f"rots{b}", 2 * JQ * NC, at=D0 + 40960 + 2048 * b)[0] for b in range(2)]
        wst, _ = place("wst", GP * 2 * P, at=HX)
        yc, _ = place("yc", GROUPS * (NC + NS), at=HX)
        u_in, _ = place("u_in", GROUPS * UW, at=D1)
        xst, _ = place("xst", GP * 2 * XW, at=D1 + 4 * GROUPS * UW)
        h_ssm, _ = place("h_ssm", KT * TOK, at=D1 + 4 * GROUPS * UW)
        y_in, _ = place("y_in", KT * TOK, at=D1)
        ones, _ = place("ones", P)
        bdiag, _ = place("bdiag", P)
        ident, _ = place("ident", P)
        ident16, _ = place("ident16", P, BF16)
        masks, _ = place("masks", 1024, BF16)
        gains, _ = place("gains", 4 * KT)
        qk_gain, _ = place("qk_gain", 2)
        dskip, _ = place("dskip", KT)
        sink, _ = place("sink", HEADS)
        nsink, _ = place("nsink", HEADS)
        sink_row, _ = place("sink_row", 1)
        nsink_row, _ = place("nsink_row", 1)
        eps, _ = place("eps", 1)
        soft, _ = place("soft", 2 * 16)
        s_soft, _ = place("s_soft", 8)
        sq = [place(f"sq{b}", TOK)[0] for b in range(2)]
        sqs, _ = place("sqs", TOK)
        rstd, _ = place("rstd", TOK)
        cw, _ = place("cw", 44 * 3)
        cb, _ = place("cb", 44)
        cbuf, _ = place("cbuf", 2 * 44 * NS)
        pre, _ = place("pre", 44 * NS)
        crow, _ = place("crow", 44 * 10)
        h0, _ = place("h0", 2 * GP * NS)
        ah0, _ = place("ah0", 2 * GP * NS)
        x_fin, _ = place("x_fin", 2 * GP)
        mag8, _ = place("mag8", GP)
        rec, REC = place("rec", JQ * 2 * P)
        ptmp, _ = place("ptmp", 2 * JQ * 64)
        bb, BB = place("bb", 2 * GP * GC)
        cc, CC = place("cc", 2 * GP * GC)
        NL = 9
        pw, _ = place("pw", NL * 2 * 2 * GP)
        rsb, _ = place("rsb", GROUPS * GC, at=BB)
        vrot = [place(f"vrot{b}", JQ * NC, at=REC + 1024 * b)[0] for b in range(2)]
        vtmp = [place(f"vtmp{b}", JQ * NC, at=REC + 2048 + 1024 * b)[0] for b in range(2)]
        zst = [place(f"zst{b}", 2 * JQ * NC, at=CC + 2048 * b)[0] for b in range(2)]
        prm, _ = place("prm", 16 * GP, at=D0 + 8192)
        braw, _ = place("braw", 2 * GP * GC, at=D0)
        btmp, _ = place("btmp", 2 * GP * GC, at=D0 + 4096)
        assert cur[0] <= nc.sbuf_usable_end, (cur[0], nc.sbuf_usable_end)

        ps = ctx.enter_context(nc.psum_tensor("ps", [P, 8, 512], F32))

        def scratch(name, shape):
            return nc.dram_tensor(name, shape, F32).ap()

        g_scr = scratch("g_scr", (NJ, P, JQ * 2 * P))
        c_scr = scratch("c_scr", (NJ, P, JQ * 2 * P))
        e_scr = scratch("e_scr", (NJ, P, 2 * JQ * NC))
        h_scr = scratch("h_scr", (D, TOK))
        y_scr = scratch("y_scr", (D, TOK))

        def tiles(t, k, n=1, w=TOK):
            return t[:, bass.ds(k * w, n * w)]

        def halves(ap):
            return ap.rearrange("p (h n) -> p h n", h=2)

        def acc(u):
            return ps[:, 2 * u:2 * u + 2, 0:HALF]

        misc = [ps[:, 4:6, 0:HALF], ps[:, 6:8, 0:HALF]]

        w_in = [sem("w_in0"), sem("w_in1")]
        hi_done, lo_done = sem("w_hi_done"), sem("w_lo_done")
        units_done, evac = sem("units_done"), sem("evac")
        sq_done, sqs_done = sem("sq_done"), sem("sqs_done")
        hx_hi_done, hx_ready = sem("hx_hi_done"), sem("hx_ready")
        stat_done, sd_done, rstd_done = sem("stat_done"), sem("sd_done"), sem("rstd_done")
        op_ready, hid_ready = sem("op_ready"), sem("hid_ready")
        consts_in, x_in, prm_in, cache_in, conv_in = (sem(n) for n in (
            "consts_in", "x_in", "prm_in", "cache_in", "conv_in"))
        conv_first, conv_done, conv_part = sem("conv_first"), sem("conv_done"), sem("conv_part")
        silu_done, hid_prod, hid_hi_done = sem("silu_done"), sem("hid_prod"), sem("hid_hi_done")
        crow_done, crow_out = sem("crow_done"), sem("crow_out")
        out_done = sem("out_done")
        n_out = [0]

        def loop(eng, n, first, body):
            for k in range(first):
                body(k)
            with eng.Fori(first, n) as k:
                body(k)

        block = ctx.enter_context(nc.Block())

        @block.sync
        def _(sp):
            def load_unit(stage, n):
                name, w, row, _, kt = INFO[stage]
                for b in range(2):
                    u = BASE[stage] + 2 * n + b
                    sp.wait_ge(lo_done, u + 1)
                    src = i[w][bass.ds(row + 2 * n + b, 1)].rearrange("o p c -> (o p) c")
                    sp.dma_start(w_raw[b][:, 0:kt * P], src).then_inc(w_in[b], 16)

            def load_stage(stage, first=0):
                with sp.Fori(first, INFO[stage][3] // 2) as n:
                    load_unit(stage, n)

            def store(dst, src):
                sp.dma_start(dst, src).then_inc(out_done, 16)
                n_out[0] += 16

            for t, name in ((ones, "ones"), (bdiag, "bdiag"), (ident, "ident"), (ident16, "ident16"),
                            (masks, "masks"), (gains, "gains"), (qk_gain, "qk_gain"), (dskip, "dskip")):
                sp.dma_start(t[:], i[name]).then_inc(consts_in, 16)
            sp.dma_start(sink[:], i["sinks"].to_broadcast([P, HEADS])).then_inc(consts_in, 16)
            for n in range(NS):
                sp.dma_start(sink_row[n * HEADS:(n + 1) * HEADS, :], i["sink_col"]).then_inc(consts_in, 16)
            sp.dma_start(x[:].rearrange("p (k t) -> p k t", k=KT),
                         i["xT"].rearrange("(k p) t -> p k t", p=P)).then_inc(x_in, 16)
            load_unit("qkv", 0)
            for n, name in enumerate(("a_re", "a_im")):
                sp.dma_start(prm[:, n * GP:(n + 1) * GP], i[name]).then_inc(prm_in, 16)
            for e in range(2):
                sp.dma_start(prm[64 * e:64 * e + 64, 2 * GP:3 * GP],
                             i["log_dt"][e:e + 1, :].to_broadcast([64, GP])).then_inc(prm_in, 16)
            for n, name in enumerate(("b_re", "b_im")):
                sp.dma_start(braw[:, n * GP * GC:(n + 1) * GP * GC], i[name]).then_inc(prm_in, 16)
            for n, name in enumerate(("c_re", "c_im")):
                sp.dma_start(cc[:, n * GP * GC:(n + 1) * GP * GC], i[name]).then_inc(prm_in, 16)
            for n, name in enumerate(("h0_re", "h0_im")):
                sp.dma_start(h0[:, n * GP * NS:(n + 1) * GP * NS], i[name]).then_inc(prm_in, 16)
            for t, name in ((cw, "conv_w"), (cb, "conv_b"), (cbuf, "conv_buf")):
                sp.dma_start(t[:], i[name][0]).then_inc(conv_in, 16)
            sp.dma_start(vc[0:P - 1, :].rearrange("t (n c) -> t n c", n=NS),
                         i["cache_v"][:, 1:P, :].rearrange("n t c -> t n c")).then_inc(cache_in, 16)
            store(o["k_sample"][:, 0:P - 1, :], i["cache_k"][:, 1:P, :])
            store(o["v_sample"][:, 0:P - 1, :], i["cache_v"][:, 1:P, :])
            load_stage("qkv", 1)
            load_unit("wo", 0)
            sp.dma_start(kc[0:P - 1, :].rearrange("t (n c) -> t n c", n=NS),
                         i["cache_k"][:, 1:P, :].rearrange("n t c -> t n c")).then_inc(sem("kc_in"), 16)
            sp.wait_ge(sem("new_rows_done"), 1)
            for n in range(NS):
                sp.dma_start(vc[P - 1:P, n * 256:(n + 1) * 256],
                             new_rows[n:n + 1, 0:256]).then_inc(sem("vc_new"), 16)
            store(o["v_sample"][:, P - 1, :], new_rows[0:NS, 0:256])
            store(o["k_sample"][:, P - 1, :], new_rows[0:NS, 256:512])
            sp.wait_ge(sem("qk_normed"), 10)
            store(o["k_prompt"], tiles(qkvT, 8, 2).rearrange("p (k t) -> p k t", k=2)[:, :, SEQ - P:SEQ])
            store(o["v_prompt"], tiles(qkvT, 10, 2).rearrange("p (k t) -> p k t", k=2)[:, :, SEQ - P:SEQ])
            sp.wait_ge(out_done, n_out[0])
            sp.sem_inc(sem("attn_stored"), 1)
            load_stage("wo", 1)
            for s in ("up00", "dn00", "up01", "dn01"):
                load_stage(s)

            def conv_out(layer):
                sp.wait_ge(crow_done, 44 * (layer + 1))
                store(o["conv_rows"][layer], crow[:])
                store(o["conv_second"][layer], cbuf[:, 44 * NS:2 * 44 * NS])

            conv_out(0)
            load_unit("glu", 0)
            sp.wait_ge(out_done, n_out[0])
            sp.sem_inc(crow_out, 1)
            for t, name in ((cw, "conv_w"), (cb, "conv_b"), (cbuf, "conv_buf")):
                sp.dma_start(t[:], i[name][1]).then_inc(conv_in, 16)

            sp.wait_ge(sem("scr_out"), 16 * 3 * NJ)
            sp.wait_ge(units_done, BASE["glu"] + 2)
            for j in range(NJ):
                if j >= 2:
                    sp.wait_ge(sem("resp_done"), j - 1)
                sp.dma_start(recs[j % 2][:], g_scr[j]).then_inc(sem(f"g_in{j % 2}"), 16)
            for k in range(KT):
                sp.wait_ge(sem("h_done"), k + 1)
                sp.dma_start(h_scr[k * P:(k + 1) * P, :], tiles(h_ssm, k)).then_inc(sem("h_out"), 16)
            sp.wait_ge(sem("h_out"), 16 * KT)
            sp.wait_ge(sem("u_zeroed"), 1)
            u3 = u_in[:].rearrange("p (g c) -> p g c", g=GROUPS)
            h3 = h_scr.rearrange("(g c) t -> c g t", c=GC)
            for s in range(CH):
                sp.dma_start(u3[GC * s:GC * (s + 1), :, NS:NS + NC],
                             h3[:, :, s * NC:(s + 1) * NC]).then_inc(sem("u_in"), 16)
            sp.dma_start(u3[0:GC, :, 0:NS], h3[:, :, SEQ:TOK]).then_inc(sem("u_in"), 16)
            sp.dma_start(u3[P - GC:P, :, NS + NC:UW], h3[:, :, SEQ:TOK]).then_inc(sem("u_in"), 16)
            sp.wait_ge(sem("rsb_done"), 1)
            sp.wait_ge(sem("toep_zeroed"), 1)
            for t in range(CH):
                n = GC * (t + 1)
                sp.dma_start(toep[0:n, t * GROUPS * GC:(t + 1) * GROUPS * GC],
                             rsb[P - n:P, :]).then_inc(sem("toep_in"), 16)
            for j in range(NJ):
                if j >= 2:
                    sp.wait_ge(sem("y_mm"), j - 1)
                    sp.wait_ge(sem("x_done"), j - 1)
                else:
                    sp.wait_ge(sem("resp_done"), NJ)
                sp.dma_start(recs[j % 2][:], c_scr[j]).then_inc(sem(f"c_in{j % 2}"), 16)
                sp.dma_start(rots[j % 2][:], e_scr[j]).then_inc(sem(f"e_in{j % 2}"), 16)
            y3 = yc[:].rearrange("p (g c) -> p g c", g=GROUPS)
            yd3 = y_scr.rearrange("(g c) t -> c g t", c=GC)
            sp.wait_ge(sem("yc_done"), NJ)
            for t in range(CH):
                sp.dma_start(yd3[:, :, t * NC:(t + 1) * NC],
                             y3[GC * t:GC * (t + 1), :, NS:NS + NC]).then_inc(sem("y_out"), 16)
            sp.dma_start(yd3[:, :, SEQ:TOK], y3[0:GC, :, 0:NS]).then_inc(sem("y_out"), 16)
            sp.wait_ge(sem("x_fin_done"), 2)
            store(o["x_fin"], x_fin[:])
            store(o["xs_new"], ah0[:])
            sp.dma_start(h_ssm[:].rearrange("p (k t) -> p k t", k=KT),
                         h_scr.rearrange("(k p) t -> p k t", p=P)).then_inc(sem("hy_in"), 16)
            sp.wait_ge(sem("y_out"), 16 * (CH + 1))
            sp.dma_start(y_in[:].rearrange("p (k t) -> p k t", k=KT),
                         y_scr.rearrange("(k p) t -> p k t", p=P)).then_inc(sem("hy_in"), 16)

            load_stage("glu", 1)
            for s in ("up10", "dn10", "up11", "dn11"):
                load_stage(s)
            conv_out(1)
            for m in range(KT):
                sp.wait_ge(evac, BASE["dn11"] + m + 3)
                store(o["yT"][m * P:(m + 1) * P, :], tiles(x, m))
            sp.wait_ge(out_done, n_out[0])

        @block.gpsimd
        def _(pool):
            pl = sem("pool_step")
            done = [0]

            def after(ins, j=None):
                done[0] += 1
                ins.then_inc(pl, 1)
                pool.wait_ge(pl, done[0] if j is None else j * per[0] + done[0])

            per = [0]

            def pre_rows():
                w3 = cw[:].rearrange("p (t j) -> p t j", j=3)
                c3 = cbuf[:].rearrange("p (r t n) -> p r t n", r=2, n=NS)
                p3 = pre[:].rearrange("p (t n) -> p t n", n=NS)
                for r, out in ((0, c3[:, 0]), (1, p3)):
                    after(pool.tensor_tensor(out, c3[:, r], w3[:, :, r:r + 1].to_broadcast([P, 44, NS]),
                                             ALU.mult))
                after(pool.tensor_tensor(p3, p3, c3[:, 0], ALU.add))
                pool.sem_inc(sem("pre_done"), 1)

            pool.wait_ge(conv_in, 48)
            pre_rows()
            pool.wait_ge(sem("bb_done"), 1)
            start = done[0]
            done[0] = 0

            def cmul(j, o_re, o_im, a_re, a_im, b_re, b_im, n, conj=False):
                t0 = ptmp[:, 0:JQ * n].rearrange("p (q n) -> p q n", q=JQ)
                t1 = ptmp[:, JQ * 64:JQ * (64 + n)].rearrange("p (q n) -> p q n", q=JQ)
                tt = pool.tensor_tensor
                after(tt(t0, a_re, b_re, ALU.mult), j)
                after(tt(t1, a_im, b_im, ALU.mult), j)
                after(tt(o_re, t0, t1, ALU.add if conj else ALU.subtract), j)
                after(tt(t0, a_im, b_re, ALU.mult), j)
                after(tt(t1, a_re, b_im, ALU.mult), j)
                after(tt(o_im, t0, t1, ALU.subtract if conj else ALU.add), j)

            def power(level, kind, j, n):
                res = []
                for ri in range(2):
                    at = ((level * 2 + ri) * 2 + kind) * GP
                    res.append(pw[:, bass.ds(at + j * JQ, JQ)].rearrange("p (q o) -> p q o", o=1)
                               .to_broadcast([P, JQ, n]))
                return res

            def tables(j):
                done[0] = start
                base_step = 0
                r5 = rec[:].rearrange("p (q r s c) -> p q r s c", q=JQ, r=2, s=CH)
                r4 = rec[:].rearrange("p (q r n) -> p q r n", q=JQ, r=2)

                def seed(src, s):
                    for ri in range(2):
                        v = src[:, bass.ds(ri * GP * GC + j * JQ * GC, JQ * GC)].rearrange(
                            "p (q c) -> p q c", q=JQ)
                        after(pool.tensor_copy(r5[:, :, ri, s, :], v), j)

                def blk(ri, s, n):
                    return r4[:, :, ri, s * GC:(s + n) * GC]

                seed(bb, CH - 1)
                for lev, dst, src, n in ((0, 6, 7, 1), (1, 4, 6, 2), (2, 0, 4, 4)):
                    pr, pi = power(lev, 0, j, n * GC)
                    cmul(j, blk(0, dst, n), blk(1, dst, n), blk(0, src, n), blk(1, src, n), pr, pi, n * GC)
                pool.dma_start(g_scr[bass.ds(j, 1)].rearrange("o p c -> (o p) c"), rec[:]).then_inc(scr, 16)
                pool.wait_ge(scr, 48 * j + 16)
                seed(cc, 0)
                pr, pi = power(0, 0, j, GC)
                cmul(j, blk(0, 1, 1), blk(1, 1, 1), blk(0, 0, 1), blk(1, 0, 1), pr, pi, GC, True)
                for ri in range(2):
                    after(pool.tensor_copy(r5[:, :, ri, 0, :], r5[:, :, ri, 1, :]), j)
                for lev, dst, src, n in ((0, 1, 0, 1), (1, 2, 0, 2), (2, 4, 0, 4)):
                    pr, pi = power(lev, 0, j, n * GC)
                    cmul(j, blk(0, dst, n), blk(1, dst, n), blk(0, src, n), blk(1, src, n), pr, pi,
                         n * GC, True)
                pool.dma_start(c_scr[bass.ds(j, 1)].rearrange("o p c -> (o p) c"), rec[:]).then_inc(scr, 16)
                pool.wait_ge(scr, 48 * j + 32)
                e4 = rec[:, 0:2 * JQ * NC].rearrange("p (r q c) -> p r q c", r=2, q=JQ)
                for ri, v in enumerate(power(3, 1, j, 1)):
                    after(pool.tensor_copy(e4[:, ri, :, 0:1], v), j)
                for lev in range(6):
                    n = 1 << lev
                    pr, pi = power(3 + lev, 1, j, n)
                    cmul(j, e4[:, 0, :, n:2 * n], e4[:, 1, :, n:2 * n], e4[:, 0, :, 0:n],
                         e4[:, 1, :, 0:n], pr, pi, n)
                pool.dma_start(e_scr[bass.ds(j, 1)].rearrange("o p c -> (o p) c"),
                               rec[:, 0:2 * JQ * NC]).then_inc(scr, 16)
                pool.wait_ge(scr, 48 * j + 48)
                assert done[0] - start == per[0], done[0] - start

            scr = sem("scr_out")
            per[0] = 2 * 4 + 6 * (3 + 1 + 3 + 6)
            for j in range(NJ):
                tables(j)
            done[0] = start + NJ * per[0]

            pool.wait_ge(units_done, BASE["glu"] + 2)
            pool.wait_ge(evac, BASE["glu"] + 2)
            u3 = u_in[:].rearrange("p (g c) -> p g c", g=GROUPS)
            pool.memset(u3[:, :, 0:NS], 0.0)
            pool.memset(u3[:, :, NS + NC:UW], 0.0).then_inc(sem("u_zeroed"), 1)
            pool.memset(toep[:], 0.0).then_inc(sem("toep_zeroed"), 1)
            pool.wait_ge(conv_in, 96)
            pre_rows()
            x4 = xst[:].rearrange("p (q r c) -> p q r c", q=GP, r=2)
            pool.wait_ge(sem("h_out"), 16 * KT)
            pool.memset(x4[:, :, :, NS:NS + 1], 0.0)
            h4 = h0[:].rearrange("p (r q n) -> p q r n", r=2, q=GP)
            for ri in range(2):
                ins = pool.tensor_copy(x4[:, :, ri, 0:NS], h4[:, :, ri, :])
            ins.then_inc(sem("x_seeded"), 1)
            for j in range(NJ):
                z = zst[j % 2][:].rearrange("p (r q c) -> p r q c", r=2, q=JQ)
                e = rots[j % 2][:].rearrange("p (r q c) -> p r q c", r=2, q=JQ)
                t0 = ptmp[:, 0:JQ * 64].rearrange("p (q c) -> p q c", q=JQ)
                t1 = ptmp[:, JQ * 64:JQ * 128].rearrange("p (q c) -> p q c", q=JQ)
                out = x4[:, JQ * j:JQ * (j + 1), :, NS + 1:NS + 1 + NC]
                pool.wait_ge(sem("z_done"), j + 1)
                tt = pool.tensor_tensor
                tt(t0, z[:, 0], e[:, 0], ALU.mult)
                after(tt(t1, z[:, 1], e[:, 1], ALU.mult))
                after(tt(out[:, :, 0, :], t0, t1, ALU.subtract))
                tt(t0, z[:, 1], e[:, 0], ALU.mult)
                after(tt(t1, z[:, 0], e[:, 1], ALU.mult))
                tt(out[:, :, 1, :], t0, t1, ALU.add).then_inc(sem("x_done"), 1)
                pool.wait_ge(sem("x_done"), j + 1)
            f3 = x_fin[:].rearrange("p (q r) -> p q r", r=2)
            pool.tensor_copy(f3.rearrange("p q (r o) -> p q r o", o=1),
                             x4[:, :, :, XW - 1:XW]).then_inc(sem("x_fin_done"), 1)

        @block.scalar
        def _(act):
            def split(u, b, kt):
                act.wait_ge(w_in[b], 8 * (u - b) + 16)
                act.wait_ge(units_done, u + 1)
                act.activation(w_hi[b][:, 0:kt * P], w_raw[b][:, 0:kt * P], ACT.Copy).then_inc(hi_done, 1)

            def norm_in(n, k, b, slots=2):
                if not (n == 0 and isinstance(k, int) and k < 2):
                    act.wait_ge(sqs_done, n * KT + k + 1 - slots)
                act.activation(sq[b][:], tiles(x, k), ACT.Square).then_inc(sq_done, 1)
                if n in HX_NORM:
                    act.activation(tiles(hx_hi, k), tiles(x, k), ACT.Copy,
                                   scale=gains[:, bass.ds(n * KT + k, 1)]).then_inc(hx_hi_done, 1)

            def norm_sd(n):
                act.wait_ge(stat_done, n + 1)
                act.activation(halves(sq[0][:]), misc[0], ACT.Sqrt, bias=eps[:]).then_inc(sd_done, 1)

            def stage(name, work, last_k=None):
                n = INFO[name][3] // 2
                kt = INFO[name][4]
                nxt = ORDER.index(name) + 1
                k_next = STAGES[nxt][4] if nxt < len(STAGES) else None

                def body(it, k):
                    for b in range(2):
                        u = BASE[name] + 2 * it + b
                        if k:
                            split(u + 2, b, k)
                        if name in NORM_OF and isinstance(it, int) and it == 0 and b == 0:
                            norm_sd(NORM_OF[name])
                        work(it, b, u)

                first = 1 if name in NORM_OF else 0
                for it in range(first):
                    body(it, kt)
                with act.Fori(first, n - 1) as it:
                    body(it, kt)
                body(n - 1, k_next)

            act.wait_ge(consts_in, 16 * 17)
            act.wait_ge(x_in, 16)
            for k in range(KT):
                norm_in(0, k, k % 2)
            split(0, 0, KT)
            split(1, 1, KT)

            act.wait_ge(prm_in, 16 * 10)
            pk = [prm[:, n * GP:(n + 1) * GP] for n in range(16)]
            act.activation(pk[2], pk[2], ACT.Exp).then_inc(sem("prm_act"), 1)
            act.wait_ge(sem("prm_dve"), 1)
            act.activation(pk[3], pk[3], ACT.Exp).then_inc(sem("prm_act"), 1)
            act.wait_ge(sem("prm_dve"), 2)
            act.activation(prm[:, 5 * GP:7 * GP], prm[:, 5 * GP:7 * GP], ACT.Sin).then_inc(sem("prm_act"), 1)

            stage("qkv", lambda it, b, u: None)

            for t in range(10):
                act.wait_ge(evac, BASE["qkv"] + t + 3)
                if t >= 2:
                    act.wait_ge(sem("qk_stat"), t - 1)
                act.activation(sq[t % 2][:], tiles(qkvT, t), ACT.Square).then_inc(sem("qk_sq"), 1)
                if t >= 1:
                    act.wait_ge(sem("qk_stat"), t)
                    if t >= 3:
                        act.wait_ge(sem("qk_normed"), t - 2)
                    act.activation(halves(qk_rms[(t - 1) % 2][:]), misc[(t - 1) % 2], ACT.Sqrt,
                                   bias=eps[:]).then_inc(sem("qk_sd"), 1)
            act.wait_ge(sem("qk_stat"), 10)
            act.wait_ge(sem("qk_normed"), 8)
            act.activation(halves(qk_rms[1][:]), misc[1], ACT.Sqrt, bias=eps[:]).then_inc(sem("qk_sd"), 1)
            act.wait_ge(sem("v_turned"), 1)
            act.activation(vtok[:].rearrange("p (b c) -> p b c", b=2), ps[:, 0:2, :],
                           ACT.Copy).then_inc(sem("vtok_done"), 1)
            act.wait_ge(sem("ks_turned"), 1)
            act.activation(ksT[:].rearrange("p (b t) -> p b t", t=P)[:, :, 0:P - 1],
                           ps[:, 4:8, :].rearrange("p b (m t) -> p (b m) t", t=P)[:, :, 0:P - 1],
                           ACT.Copy).then_inc(sem("ksT_done"), 1)
            act.wait_ge(sem("s_scored"), 1)
            act.activation(s_st[:].rearrange("p (m e g) -> p e m g", e=2, g=4),
                           ps[:, 2:4, 0:64].rearrange("p e (m g) -> p e m g", g=4),
                           ACT.Copy).then_inc(sem("s_st_done"), 1)
            act.wait_ge(sem("s_maxed"), 1)
            act.activation(s_pr[:], ps[:, 0, 0:P], ACT.Exp, bias=s_soft[:, 1:2], scale=SCALE,
                           accum_out=s_soft[:, 2:3])
            act.activation(s_soft[:, 3:4], s_soft[:, 1:2], ACT.Exp, bias=sink_row[:]).then_inc(sem("s_exp"), 1)
            act.wait_ge(sem("s_pturned"), 1)
            act.activation(s_pT[:], ps[:, 1, 0:P], ACT.Copy).then_inc(sem("s_pT_done"), 1)
            act.wait_ge(sem("s_out"), 1)
            act.activation(op_hi[:].rearrange("p (k t) -> p k t", k=KT)[:, :, SEQ:TOK],
                           ps[:, 2, 0:NS * KT].rearrange("p (n k) -> p k n", n=NS),
                           ACT.Copy).then_inc(sem("o_hi"), 1)

            def attn_exp(a):
                b = a % 2
                act.wait_ge(sem("maxed"), a + 1)
                if a >= 2:
                    act.wait_ge(sem("p_turned"), a - 1)
                for blk in range(NB):
                    lo = P if blk == 0 else 0
                    act.activation(probs[b][:, blk * 256 + lo:(blk + 1) * 256],
                                   ps[:, 2 * b + blk // 2, (blk % 2) * 256 + lo:(blk % 2) * 256 + 256],
                                   ACT.Exp, bias=soft[:, 16 * b + 4 + blk:16 * b + 5 + blk], scale=SCALE,
                                   accum_out=soft[:, 16 * b + 8 + blk:16 * b + 9 + blk])
                act.activation(soft[:, 16 * b + 12:16 * b + 16], soft[:, 16 * b + 4:16 * b + 8], ACT.Exp,
                               bias=sink[:, a_head(a):a_head(a) + 1]).then_inc(sem("exp_done"), 1)

            def attn_turn(a):
                act.wait_ge(sem("p_turned"), a + 1)
                if a >= 2:
                    act.wait_ge(sem("pv_done"), a - 1)
                act.activation(probsT[a % 2][:, 0:512], ps[:, 4, :], ACT.Copy).then_inc(sem("pT_act"), 1)

            def attn_out(a):
                if a % 2:
                    act.wait_ge(sem("pv_done"), a + 1)
                    act.activation(tiles(op_hi, a // 2)[:, 0:SEQ], ps[:, 6 + (a // 2) % 2, :],
                                   ACT.Copy).then_inc(sem("o_hi"), 1)

            attn_exp(0)
            for a in range(HEADS):
                if a + 1 < HEADS:
                    attn_exp(a + 1)
                attn_turn(a)
                if a >= 1:
                    attn_out(a - 1)
            attn_out(HEADS - 1)

            def residual(n):
                def work(it, b, u):
                    act.wait_ge(evac, u + 3)
                    norm_in(n, 2 * it + b, b)
                return work

            def ffn(layer, half):
                tb = 44 * layer
                hb = (2 * layer + half) * NPAIR

                def up(it, b, u):
                    t = 2 * it + b + 22 * half
                    if b == 1:
                        act.wait_ge(conv_done, 2 * (hb + it) + 1)
                        if not (hb == 0 and isinstance(it, int) and it == 0):
                            act.wait_ge(hid_prod, hb + it)
                        act.activation(silu_g[:], conv[0][:], ACT.Silu).then_inc(silu_done, 1)
                    act.wait_ge(evac, u + 3)
                    act.activation(crow[:, bass.ds(t * 10, 10)], up_row[b][:, UCOL - 10:UCOL],
                                   ACT.Copy).then_inc(crow_done, 1)
                    if not (hb == 0 and isinstance(it, int) and it == 0):
                        act.wait_ge(hid_prod, hb + it)
                    act.activation(conv[b][:], up_row[b][:, 2:UCOL], ACT.Identity,
                                   scale=cw[:, bass.ds(t * 3 + 2, 1)],
                                   bias=cb[:, bass.ds(t, 1)]).then_inc(conv_first, 1)
                    if b == 1:
                        act.wait_ge(hid_prod, hb + it + 1)
                        act.activation(tiles(hid_hi, it), hid[:], ACT.Copy).then_inc(hid_hi_done, 1)

                if layer == 0 and half == 0:
                    act.wait_ge(sem("attn_stored"), 1)
                if layer == 1 and half == 0:
                    act.wait_ge(crow_out, 1)
                    act.wait_ge(conv_in, 96)
                stage(f"up{layer}{half}", up)
                stage(f"dn{layer}{half}", residual(2) if (layer, half) == (0, 1) else (lambda it, b, u: None))

            stage("wo", residual(1))
            ffn(0, 0)
            ffn(0, 1)

            norm_sd(2)
            for j in range(NJ):
                act.wait_ge(sem("resp_done"), j + 1)
                act.activation(wst[:, j * 1024:j * 1024 + 512], ps[:, 2 * (j % 2), :],
                               ACT.Copy).then_inc(sem("wst_act"), 1)
            act.activation(rsb[:].rearrange("p (c q e) -> p e q c", c=GC, e=2),
                           ps[:, 6:8, :].rearrange("p e (q c) -> p e q c", c=GC),
                           ACT.Copy).then_inc(sem("rsb_done"), 1)
            for j in range(NJ):
                act.wait_ge(sem("y_mm"), j + 1)
                act.activation(yc[:, j * 576:(j + 1) * 576].rearrange("p (q e c) -> p e q c", q=JQ, e=2),
                               ps[:, 4 + 2 * (j % 2):6 + 2 * (j % 2), 0:288].rearrange("p e (q c) -> p e q c", q=JQ),
                               ACT.Copy).then_inc(sem("yc_done"), 1)
            for k in range(KT):
                act.wait_ge(sem("yd_done"), k + 1)
                zf = sq[k % 2]
                if k >= 2:
                    act.wait_ge(op_ready, 9 + k - 1)
                act.activation(zf[:, 0:SEQ].rearrange("p (c s) -> p s c", s=CH),
                               tiles(y_in, k)[:, 0:SEQ].rearrange("p (s c) -> p s c", s=CH),
                               ACT.Gelu_apprx_tanh)
                act.activation(zf[:, SEQ:TOK], tiles(y_in, k)[:, SEQ:TOK],
                               ACT.Gelu_apprx_tanh).then_inc(sem("z_gelu"), 1)
                act.wait_ge(sem("z_gelu"), k + 1)
                act.activation(tiles(op_hi, k), zf[:], ACT.Copy).then_inc(sem("z_hi"), 1)

            prepare3 = residual(3)

            def glu(it, b, u):
                if b == 1:
                    act.wait_ge(units_done, u + 3)
                    act.wait_ge(evac, u + 2)
                    act.activation(halves(conv[1][:]), acc(1), ACT.Tanh, scale=0.5).then_inc(sem("tanh_done"), 1)
                    act.wait_ge(sem("glu_done"), it + 1)
                    norm_in(3, it, 0, slots=1)

            stage("glu", glu)
            ffn(1, 0)
            ffn(1, 1)

        @block.vector
        def _(dve):
            dv = sem("dve_step")
            done = [0]

            def after(ins):
                done[0] += 1
                ins.then_inc(dv, 1)
                dve.wait_ge(dv, done[0])

            def split(u, b, kt):
                dve.wait_ge(hi_done, u + 1)
                dve.tensor_tensor(w_lo[b][:, 0:kt * P], w_raw[b][:, 0:kt * P],
                                  w_hi[b][:, 0:kt * P].bitcast(F32), ALU.subtract).then_inc(lo_done, 1)

            def norm_in(n, k, b, first=False):
                dve.wait_ge(sq_done, n * KT + k + 1)
                if first:
                    dve.tensor_copy(sqs[:], sq[b][:]).then_inc(sqs_done, 1)
                else:
                    dve.wait_ge(sqs_done, n * KT + k)
                    dve.tensor_tensor(sqs[:], sqs[:], sq[b][:], ALU.add).then_inc(sqs_done, 1)
                if n in HX_NORM:
                    dve.wait_ge(hx_hi_done, HX_NORM[n] * KT + k + 1)
                    dve.scalar_tensor_tensor(tiles(hx_lo, k), tiles(x, k), gains[:, bass.ds(n * KT + k, 1)],
                                             tiles(hx_hi, k).bitcast(F32), ALU.mult,
                                             ALU.subtract).then_inc(hx_ready, 1)

            def norm_rstd(n):
                dve.wait_ge(sd_done, n + 1)
                dve.reciprocal(rstd[:], sq[0][:]).then_inc(rstd_done, 1)
                dve.wait_ge(rstd_done, n + 1)

            def stage(name, work):
                n = INFO[name][3] // 2
                kt = INFO[name][4]
                nxt = ORDER.index(name) + 1
                k_next = STAGES[nxt][4] if nxt < len(STAGES) else None

                def body(it, k):
                    for b in range(2):
                        u = BASE[name] + 2 * it + b
                        if k:
                            split(u + 2, b, k)
                        if name in NORM_OF and isinstance(it, int) and it == 0 and b == 0:
                            norm_rstd(NORM_OF[name])
                        work(it, b, u)

                first = 1 if name in NORM_OF or name in PREPARES else 0
                for it in range(first):
                    body(it, kt)
                with dve.Fori(first, n - 1) as it:
                    body(it, kt)
                body(n - 1, k_next)

            dve.memset(eps[:], EPS)
            dve.sem_inc(lo_done, 2)
            dve.sem_inc(evac, 2)
            after(dve.memset(soft[:], 0.0))
            dve.wait_ge(consts_in, 16 * 17)
            dve.tensor_scalar(nsink[:], sink[:], -1.0, None, ALU.mult)
            after(dve.tensor_scalar(nsink_row[:], sink_row[:], -1.0, None, ALU.mult))
            for k in range(KT):
                norm_in(0, k, k % 2, k == 0)
            split(0, 0, KT)
            split(1, 1, KT)

            pk = [prm[:, n * GP:(n + 1) * GP] for n in range(16)]
            a_re, a_im, dt = pk[0], pk[1], pk[2]
            tt, ts, stt = dve.tensor_tensor, dve.tensor_scalar, dve.scalar_tensor_tensor
            dve.wait_ge(prm_in, 160)
            dve.wait_ge(sem("prm_act"), 1)
            tt(pk[3], a_re, dt, ALU.mult).then_inc(sem("prm_dve"), 1)
            after(tt(pk[4], a_im, dt, ALU.mult))
            after(ts(pk[5], pk[4], 1.0 / (2 * PI), MAGIC, ALU.mult, ALU.add))
            after(ts(pk[6], pk[4], 1.0 / (2 * PI), 0.25, ALU.mult, ALU.add))
            after(ts(pk[6], pk[6], MAGIC, None, ALU.add))
            after(ts(prm[:, 7 * GP:9 * GP], prm[:, 5 * GP:7 * GP], MAGIC, None, ALU.subtract))
            TURN = 6.28125
            for n in range(2):
                after(stt(pk[5 + n], pk[7 + n], -TURN, pk[4], ALU.mult, ALU.add))
                after(stt(pk[5 + n], pk[7 + n], -(2 * PI - TURN), pk[5 + n], ALU.mult, ALU.add))
            after(ts(pk[6], pk[6], PI / 2, None, ALU.add))
            ts(prm[:, 5 * GP:7 * GP], prm[:, 5 * GP:7 * GP], 3.1415925, -3.1415925, ALU.min,
               ALU.max).then_inc(sem("prm_dve"), 1)
            dve.wait_ge(sem("prm_act"), 3)
            pv = pw[:].rearrange("p (l r k q) -> p l r k q", l=NL, r=2, k=2)
            tt(pv[:, 0, 0, 0], pk[3], pk[6], ALU.mult)
            tt(pv[:, 0, 1, 0], pk[3], pk[5], ALU.mult)
            dve.tensor_copy(pv[:, 0, 0, 1], pk[6])
            after(dve.tensor_copy(pv[:, 0, 1, 1], pk[5]))
            m = prm[:, 9 * GP:11 * GP].rearrange("p (k q) -> p k q", k=2)
            m2 = prm[:, 11 * GP:13 * GP].rearrange("p (k q) -> p k q", k=2)
            for lev in range(1, NL):
                re, im = pv[:, lev - 1, 0], pv[:, lev - 1, 1]
                tt(m, re, re, ALU.mult)
                tt(m2, im, im, ALU.mult)
                after(stt(pv[:, lev, 1], re, 2.0, im, ALU.mult, ALU.mult))
                after(tt(pv[:, lev, 0], m, m2, ALU.subtract))
            after(tt(mag8[:], pk[3], pk[3], ALU.mult))
            after(tt(mag8[:], mag8[:], mag8[:], ALU.mult))
            after(tt(mag8[:], mag8[:], mag8[:], ALU.mult))
            tt(pk[9], a_re, a_re, ALU.mult)
            after(tt(pk[10], a_im, a_im, ALU.mult))
            after(tt(pk[9], pk[9], pk[10], ALU.add))
            after(dve.reciprocal(pk[10], pk[9]))
            after(ts(pk[11], pv[:, 0, 0, 0], -1.0, None, ALU.add))
            tt(pk[12], pk[11], a_re, ALU.mult)
            after(tt(pk[13], pv[:, 0, 1, 0], a_im, ALU.mult))
            after(tt(pk[12], pk[12], pk[13], ALU.add))
            tt(pk[14], pv[:, 0, 1, 0], a_re, ALU.mult)
            after(tt(pk[15], pk[11], a_im, ALU.mult))
            after(tt(pk[13], pk[14], pk[15], ALU.subtract))
            after(tt(pk[12], pk[12], pk[10], ALU.mult))
            after(tt(pk[13], pk[13], pk[10], ALU.mult))

            def wide(ap, n):
                return ap.rearrange("p (q o) -> p q o", o=1).to_broadcast([P, GP, n])

            def cmul(out, a_r, a_i, src, n):
                s4 = src[:].rearrange("p (r q c) -> p r q c", r=2, q=GP)
                o4 = out[:].rearrange("p (r q c) -> p r q c", r=2, q=GP)
                t4 = btmp[:, 0:2 * GP * n].rearrange("p (r q c) -> p r q c", r=2, q=GP)
                tt(t4[:, 0], s4[:, 0], a_r, ALU.mult)
                after(tt(t4[:, 1], s4[:, 1], a_i, ALU.mult))
                after(tt(o4[:, 0], t4[:, 0], t4[:, 1], ALU.subtract))
                tt(t4[:, 0], s4[:, 1], a_r, ALU.mult)
                after(tt(t4[:, 1], s4[:, 0], a_i, ALU.mult))
                after(tt(o4[:, 1], t4[:, 0], t4[:, 1], ALU.add))

            cmul(bb, wide(pk[12], GC), wide(pk[13], GC), braw, GC)
            cmul(ah0, wide(pv[:, 0, 0, 0], NS), wide(pv[:, 0, 1, 0], NS), h0, NS)
            after(ts(cc[:, GP * GC:2 * GP * GC], cc[:, GP * GC:2 * GP * GC], -1.0, None, ALU.mult))
            dve.sem_inc(sem("bb_done"), 1)

            def qkv(it, b, u):
                dve.wait_ge(units_done, u + 3)
                dve.tensor_tensor(halves(tiles(qkvT, 2 * it + b)), acc(b), halves(rstd[:]),
                                  ALU.mult).then_inc(evac, 1)

            stage("qkv", qkv)
            for t in range(10):
                dve.wait_ge(sem("qk_sd"), t + 1)
                after(dve.reciprocal(qk_rms[t % 2][:], qk_rms[t % 2][:]))
                g = 0 if t < 8 else 1
                stt(tiles(qkvT, t), tiles(qkvT, t), qk_gain[:, g:g + 1], qk_rms[t % 2][:], ALU.mult,
                    ALU.mult).then_inc(sem("qk_normed"), 1)
            dve.wait_ge(sem("rows_turned"), 1)
            dve.tensor_copy(new_rows[0:NS, :], ps[0:NS, 2, :]).then_inc(sem("new_rows_done"), 1)
            dve.wait_ge(sem("qk_normed"), 10)
            dve.tensor_copy(ksT[:].rearrange("p (n k t) -> p n k t", n=NS, k=2)[:, :, :, P - 1:P],
                            tiles(qkvT, 8, 2).rearrange("p (k t o) -> p t k o", k=2, o=1)[:, SEQ:TOK]
                            ).then_inc(sem("ksT_new"), 1)
            dve.wait_ge(sem("s_turned"), 1)
            after(dve.tensor_reduce(s_soft[:, 0:1], ps[:, 0, 0:P], AX.X, ALU.max))
            ts(s_soft[:, 1:2], s_soft[:, 0:1], -SCALE, nsink_row[:], ALU.mult, ALU.min).then_inc(sem("s_maxed"), 1)
            dve.wait_ge(sem("s_exp"), 1)
            after(tt(s_soft[:, 4:5], s_soft[:, 2:3], s_soft[:, 3:4], ALU.add))
            after(dve.reciprocal(s_soft[:, 5:6], s_soft[:, 4:5]))
            ts(s_pr[:], s_pr[:], s_soft[:, 5:6], None, ALU.mult).then_inc(sem("s_pr_done"), 1)
            dve.wait_ge(sem("o_hi"), 1)
            sc = ps[:, 2, 0:NS * KT].rearrange("p (n k) -> p k n", n=NS)
            tt(op_lo[:].rearrange("p (k t) -> p k t", k=KT)[:, :, SEQ:TOK], sc,
               op_hi[:].bitcast(F32).rearrange("p (k t) -> p k t", k=KT)[:, :, SEQ:TOK],
               ALU.subtract).then_inc(op_ready, 1)

            def attn_max(a):
                b = a % 2
                dve.wait_ge(sem("scored"), a + 1)
                after(dve.tensor_reduce(soft[:, 16 * b:16 * b + 4],
                                        ps[:, 2 * b:2 * b + 2, :].rearrange("p b (m c) -> p b m c", m=2),
                                        AX.X, ALU.max))
                h = a_head(a)
                ts(soft[:, 16 * b + 4:16 * b + 8], soft[:, 16 * b:16 * b + 4], -SCALE, nsink[:, h:h + 1],
                   ALU.mult, ALU.min).then_inc(sem("maxed"), 1)

            def attn_norm(a):
                b = a % 2
                dve.wait_ge(sem("exp_done"), a + 1)
                s = soft[:, 16 * b:16 * b + 16]
                after(tt(s[:, 8:12], s[:, 8:12], s[:, 12:16], ALU.add))
                after(dve.reciprocal(s[:, 12:16], s[:, 8:12]))
                for blk in range(NB):
                    lo = P if blk == 0 else 0
                    v = probs[b][:, blk * 256 + lo:(blk + 1) * 256]
                    ins = ts(v, v, s[:, 12 + blk:13 + blk], None, ALU.mult)
                ins.then_inc(sem("p_done"), 1)

            def attn_turn(a):
                dve.wait_ge(sem("p_turned"), a + 1)
                if a >= 2:
                    dve.wait_ge(sem("pv_done"), a - 1)
                dve.tensor_copy(probsT[a % 2][:, 512:896], ps[:, 5, 0:384]).then_inc(sem("pT_dve"), 1)

            def attn_out(a):
                if a % 2:
                    j = a // 2
                    dve.wait_ge(sem("o_hi"), j + 2)
                    tt(tiles(op_lo, j)[:, 0:SEQ], ps[:, 6 + j % 2, :], tiles(op_hi, j)[:, 0:SEQ].bitcast(F32),
                       ALU.subtract).then_inc(op_ready, 1)

            attn_max(0)
            attn_norm(0)
            for a in range(HEADS):
                if a + 1 < HEADS:
                    attn_max(a + 1)
                attn_turn(a)
                if a + 1 < HEADS:
                    attn_norm(a + 1)
                if a >= 1:
                    attn_out(a - 1)
            attn_out(HEADS - 1)

            def residual(n=None):
                def work(it, b, u):
                    m = 2 * it + b
                    dve.wait_ge(units_done, u + 3)
                    tt(halves(tiles(x, m)), acc(b), halves(tiles(x, m)), ALU.add).then_inc(evac, 1)
                    if n is not None:
                        norm_in(n, m, b, isinstance(it, int) and m == 0)
                return work

            def ffn(layer, half):
                hb = (2 * layer + half) * NPAIR
                if half == 0:
                    dve.wait_ge(sem("pre_done"), layer + 1)
                    if layer == 0:
                        dve.wait_ge(sem("attn_stored"), 1)
                    for b in range(2):
                        ins = dve.memset(up_row[b][:, 0:2], 0.0)
                    after(ins)

                def up(it, b, u):
                    t = 2 * it + b + 22 * half
                    n = 2 * (hb + it) + b
                    dve.wait_ge(units_done, u + 3)
                    if not (hb == 0 and isinstance(it, int) and it == 0):
                        dve.wait_ge(conv_first, n - 1)
                        dve.wait_ge(conv_done, n - 1)
                    tt(halves(up_row[b][:, 2:UCOL]), acc(b), halves(rstd[:]), ALU.mult).then_inc(evac, 1)
                    dve.wait_ge(conv_first, n + 1)
                    c = conv[b]
                    stt(c[:, 0:SEQ], up_row[b][:, 0:SEQ], cw[:, bass.ds(t * 3, 1)], c[:, 0:SEQ],
                        ALU.mult, ALU.add).then_inc(conv_part, 1)
                    tt(c[:, SEQ:TOK], c[:, SEQ:TOK], pre[:, bass.ds(t * NS, NS)], ALU.add)
                    dve.wait_ge(conv_part, n + 1)
                    stt(c[:, 0:SEQ], up_row[b][:, 1:1 + SEQ], cw[:, bass.ds(t * 3 + 1, 1)], c[:, 0:SEQ],
                        ALU.mult, ALU.add).then_inc(conv_done, 1)
                    if b == 1:
                        dve.wait_ge(silu_done, hb + it + 1)
                        dve.wait_ge(conv_done, n + 1)
                        if not (hb == 0 and isinstance(it, int) and it == 0):
                            dve.wait_ge(hid_ready, hb + it)
                        tt(hid[:], silu_g[:], c[:], ALU.mult).then_inc(hid_prod, 1)
                        dve.wait_ge(hid_hi_done, hb + it + 1)
                        dve.wait_ge(hid_prod, hb + it + 1)
                        tt(tiles(hid_lo, it), hid[:], tiles(hid_hi, it).bitcast(F32),
                           ALU.subtract).then_inc(hid_ready, 1)

                stage(f"up{layer}{half}", up)
                stage(f"dn{layer}{half}", residual(2 if (layer, half) == (0, 1) else None))

            stage("wo", residual(1))
            ffn(0, 0)
            ffn(0, 1)

            norm_rstd(2)
            for k in range(KT):
                g = gains[:, 2 * KT + k:2 * KT + k + 1]
                hk, xk = tiles(h_ssm, k), tiles(x, k)
                stt(hk[:, 0:SEQ].rearrange("p (s c) -> p s c", s=CH),
                    xk[:, 0:SEQ].rearrange("p (c s) -> p s c", s=CH), g,
                    rstd[:, 0:SEQ].rearrange("p (c s) -> p s c", s=CH), ALU.mult, ALU.mult)
                stt(hk[:, SEQ:TOK], xk[:, SEQ:TOK], g, rstd[:, SEQ:TOK], ALU.mult,
                    ALU.mult).then_inc(sem("h_done"), 1)
            for j in range(NJ):
                dve.wait_ge(sem("resp_done"), j + 1)
                dve.tensor_copy(wst[:, j * 1024 + 512:(j + 1) * 1024],
                                ps[:, 2 * (j % 2) + 1, :]).then_inc(sem("wst_dve"), 1)
            a4 = ah0[:].rearrange("p (r q n) -> p r q n", r=2, q=GP)
            for j in range(NJ):
                b = j % 2
                v = [ps[:, 2 * b + ri, 0:288].rearrange("p (q c) -> p q c", q=JQ) for ri in range(2)]
                e = rots[b][:].rearrange("p (r q c) -> p r q c", r=2, q=JQ)
                vr = [t[:].rearrange("p (q c) -> p q c", q=JQ) for t in vrot]
                vt = [t[:].rearrange("p (q c) -> p q c", q=JQ) for t in vtmp]
                dve.wait_ge(sem("v_done"), j + 1)
                dve.wait_ge(sem(f"e_in{b}"), 16 * (j // 2 + 1))
                tt(vt[0], v[0][:, :, 0:NC], e[:, 0], ALU.mult)
                after(tt(vt[1], v[1][:, :, 0:NC], e[:, 1], ALU.mult))
                after(tt(vr[0], vt[0], vt[1], ALU.add))
                tt(vt[0], v[1][:, :, 0:NC], e[:, 0], ALU.mult)
                after(tt(vt[1], v[0][:, :, 0:NC], e[:, 1], ALU.mult))
                after(tt(vr[1], vt[0], vt[1], ALU.subtract))
                for ri in range(2):
                    ins = tt(a4[:, ri, JQ * j:JQ * (j + 1), :], v[ri][:, :, NC:NC + NS],
                             a4[:, ri, JQ * j:JQ * (j + 1), :], ALU.add)
                ins.then_inc(sem("v_used"), 1)
                if j >= 2:
                    dve.wait_ge(sem("x_done"), j - 1)
                for ri in range(2):
                    for q in range(JQ):
                        at = (ri * JQ + q) * NC
                        ins = dve.tensor_tensor_scan(
                            zst[b][:, at:at + NC],
                            mag8[:, JQ * j + q:JQ * j + q + 1].to_broadcast([P, NC]),
                            vrot[ri][:, q * NC:(q + 1) * NC], 0.0, ALU.mult, ALU.add)
                ins.then_inc(sem("z_done"), 1)
                dve.wait_ge(sem("z_done"), j + 1)
            dve.wait_ge(sem("v_used"), NJ)
            dve.sem_inc(sem("x_fin_done"), 1)
            dve.wait_ge(sem("hy_in"), 32)
            for k in range(KT):
                stt(tiles(y_in, k), tiles(h_ssm, k), dskip[:, k:k + 1], tiles(y_in, k), ALU.mult,
                    ALU.add).then_inc(sem("yd_done"), 1)
            for k in range(KT):
                dve.wait_ge(sem("z_hi"), k + 1)
                tt(tiles(op_lo, k), sq[k % 2][:], tiles(op_hi, k).bitcast(F32),
                   ALU.subtract).then_inc(op_ready, 1)

            def glu(it, b, u):
                dve.wait_ge(units_done, u + 3)
                if b == 0:
                    dve.tensor_copy(halves(conv[0][:]), acc(0)).then_inc(evac, 1)
                    dve.wait_ge(evac, u + 3)
                else:
                    dve.wait_ge(sem("tanh_done"), it + 1)
                    stt(hid[:], conv[1][:], 1.0, conv[0][:], ALU.add, ALU.mult).then_inc(evac, 1)
                    dve.wait_ge(evac, u + 3)
                    stt(tiles(x, it), hid[:], 0.5, tiles(x, it), ALU.mult, ALU.add).then_inc(sem("glu_done"), 1)
                    dve.wait_ge(sem("glu_done"), it + 1)
                    norm_in(3, it, 0, isinstance(it, int) and it == 0)

            stage("glu", glu)
            ffn(1, 0)
            ffn(1, 1)

        @block.tensor
        def _(pe):
            def unit(stage, n, b, hi, lo, kwait=None):
                kt = INFO[stage][4]
                u = BASE[stage] + 2 * n + b
                pe.wait_ge(lo_done, u + 3)
                pe.wait_ge(evac, u + 1)
                for k in range(kt):
                    if kwait:
                        pe.wait_ge(kwait[0], kwait[1] + k + 1)
                    wh, wl = w_hi[b][:, k * P:(k + 1) * P], w_lo[b][:, k * P:(k + 1) * P]
                    for h in range(2):
                        c0 = k * TOK + h * HALF
                        xh, xl = hi[:, c0:c0 + HALF], lo[:, c0:c0 + HALF]
                        out = ps[:, 2 * b + h, 0:HALF]
                        pe.matmul(out, wh, xh, start=(k == 0), stop=False)
                        pe.matmul(out, wh, xl, start=False, stop=False)
                        ins = pe.matmul(out, wl, xh, start=False, stop=(k == kt - 1))
                ins.then_inc(units_done, 1)

            def norm_stat(n):
                pe.wait_ge(sqs_done, KT * (n + 1))
                for h in range(2):
                    ins = pe.matmul(misc[0][:, h], ones[:], sqs[:, h * HALF:(h + 1) * HALF],
                                    start=True, stop=True)
                ins.then_inc(stat_done, 1)

            def stage(name, hi, lo, ready):
                unit(name, 0, 0, hi, lo, ready)
                if name in NORM_OF:
                    norm_stat(NORM_OF[name])
                unit(name, 0, 1, hi, lo)
                with pe.Fori(1, INFO[name][3] // 2) as n:
                    for b in range(2):
                        unit(name, n, b, hi, lo)

            pe.sem_inc(units_done, 2)
            pe.wait_ge(consts_in, 16 * 17)
            stage("qkv", hx_hi, hx_lo, (hx_ready, 0))

            for t in range(10):
                pe.wait_ge(sem("qk_sq"), t + 1)
                if t >= 2:
                    pe.wait_ge(sem("qk_sd"), t - 1)
                elif t == 0:
                    pe.wait_ge(sd_done, 1)
                for h in range(2):
                    ins = pe.matmul(misc[t % 2][:, h], bdiag[:], sq[t % 2][:, h * HALF:(h + 1) * HALF],
                                    start=True, stop=True)
                ins.then_inc(sem("qk_stat"), 1)

            def qt(t, c0, n, e=None):
                rows = slice(0, P) if e is None else slice(64 * e, 64 * e + 64)
                return qkvT[rows, t * TOK + c0:t * TOK + c0 + n]

            pe.wait_ge(evac, BASE["wo"] + 2)
            for blk in range(NB):
                for v in range(2):
                    ins = pe.transpose(ps[:, blk // 2, (blk % 2) * 256 + v * P:(blk % 2) * 256 + (v + 1) * P],
                                       qt(10 + v, blk * P, P), ident[:])
            ins.then_inc(sem("v_turned"), 1)
            pe.wait_ge(sem("qk_normed"), 10)
            for v in range(4):
                ins = pe.transpose(ps[0:NS, 2, v * P:(v + 1) * P], qt((10, 11, 8, 9)[v], SEQ, NS), ident[:])
            ins.then_inc(sem("rows_turned"), 1)
            pe.wait_ge(sem("kc_in"), 16)
            pe.wait_ge(sem("qk_sd"), 10)
            for n in range(NS):
                for p in range(2):
                    m = 2 * n + p
                    ins = pe.transpose(ps[:, 4 + m // 4, (m % 4) * P:(m % 4) * P + P - 1],
                                       kc[0:P - 1, n * 256 + p * P:n * 256 + (p + 1) * P],
                                       ident[0:P - 1, 0:P - 1])
            ins.then_inc(sem("ks_turned"), 1)
            pe.wait_ge(sem("new_rows_done"), 1)
            pe.wait_ge(sem("ksT_done"), 1)
            pe.wait_ge(sem("ksT_new"), 1)
            q3 = qkvT[:].rearrange("p (t c) -> p t c", t=12)
            for n in range(NS):
                for p in range(2):
                    for e in range(2):
                        r = slice(64 * e, 64 * e + 64)
                        c0 = n * 8 + p * 4
                        ins = pe.matmul(ps[:, 2 + e, c0:c0 + 4], ksT[r, (2 * n + p) * P:(2 * n + p + 1) * P],
                                        q3[r, 4 * p:4 * p + 4, SEQ + n], start=True, stop=True)
            ins.then_inc(sem("s_scored"), 1)
            pe.wait_ge(sem("s_st_done"), 1)
            pe.wait_ge(sem("vtok_done"), 1)
            pe.transpose(ps[:, 0, 0:P], s_st[:], ident[:]).then_inc(sem("s_turned"), 1)
            pe.wait_ge(sem("s_pr_done"), 1)
            pe.transpose(ps[:, 1, 0:P], s_pr[:], ident[:]).then_inc(sem("s_pturned"), 1)
            pe.wait_ge(sem("s_pT_done"), 1)
            pe.wait_ge(sem("vc_new"), 16 * NS)
            pe.wait_ge(cache_in, 16)
            pe.wait_ge(sem("new_rows_done"), 1)
            for n in range(NS):
                for p in range(2):
                    for e in range(2):
                        c0 = n * HEADS + p * 8 + e * 4
                        kv = 2 * p + e
                        ins = pe.matmul(ps[64 * e:64 * e + 64, 2, n * KT + 4 * p:n * KT + 4 * p + 4],
                                        vc[:, n * 256 + kv * HD:n * 256 + (kv + 1) * HD],
                                        s_pT[:, c0:c0 + 4], start=True, stop=True)
            ins.then_inc(sem("s_out"), 1)

            def scores(a):
                b, (p, g, e) = a % 2, a_split(a)
                if a >= 2:
                    pe.wait_ge(sem("exp_done"), a - 1)
                elif a == 0:
                    pe.wait_ge(sem("s_pT_done"), 1)
                else:
                    pe.wait_ge(op_ready, 1)
                r = slice(64 * e, 64 * e + 64)
                for bank in range(2):
                    pe.matmul(ps[:, 2 * b + bank, :], ident16[:], masks[:, bank * 512:(bank + 1) * 512],
                              start=True, stop=False, skip_group_check=True)
                    for blk in (2 * bank, 2 * bank + 1):
                        k0 = max(blk - 1, 0)
                        w = (blk - k0 + 1) * P
                        c1 = (blk % 2) * 256 + 256
                        ins = pe.matmul(ps[:, 2 * b + bank, c1 - w:c1],
                                        qkvT[r, (4 * p + g) * TOK + blk * P:(4 * p + g) * TOK + (blk + 1) * P],
                                        qkvT[r, (8 + p) * TOK + k0 * P:(8 + p) * TOK + k0 * P + w],
                                        start=False, stop=(blk % 2 == 1), skip_group_check=True)
                ins.then_inc(sem("scored"), 1)

            def turn(a):
                b = a % 2
                pe.wait_ge(sem("p_done"), a + 1)
                if a >= 1:
                    pe.wait_ge(sem("pT_act"), a)
                    pe.wait_ge(sem("pT_dve"), a)
                else:
                    pe.wait_ge(sem("ksT_done"), 1)
                for blk in range(NB):
                    for prev in ((0,) if blk == 0 else (1, 0)):
                        slot = 2 * blk - prev
                        c0 = blk * 256 + (0 if prev else P)
                        ins = pe.transpose(ps[:, 4 + slot // 4, (slot % 4) * P:(slot % 4) * P + P],
                                           probs[b][:, c0:c0 + P], ident[:])
                ins.then_inc(sem("p_turned"), 1)

            def pv(a):
                b, (p, g, e) = a % 2, a_split(a)
                pe.wait_ge(sem("pT_act"), a + 1)
                pe.wait_ge(sem("pT_dve"), a + 1)
                j = a // 2
                if e == 0 and j >= 2:
                    pe.wait_ge(op_ready, j)
                kv = 2 * p + e
                for blk in range(NB):
                    for prev in ((0,) if blk == 0 else (1, 0)):
                        slot = 2 * blk - prev
                        ins = pe.matmul(ps[64 * e:64 * e + 64, 6 + j % 2, blk * P:(blk + 1) * P],
                                        vtok[:, (blk - prev) * 256 + kv * HD:(blk - prev) * 256 + (kv + 1) * HD],
                                        probsT[b][:, slot * P:(slot + 1) * P],
                                        start=(prev == 1 or blk == 0), stop=(prev == 0))
                ins.then_inc(sem("pv_done"), 1)

            scores(0)
            for a in range(HEADS):
                if a + 1 < HEADS:
                    scores(a + 1)
                turn(a)
                pv(a)

            pe.wait_ge(op_ready, 9)
            stage("wo", op_hi, op_lo, (op_ready, 1))
            stage("up00", hx_hi, hx_lo, (hx_ready, KT))
            stage("dn00", hid_hi, hid_lo, (hid_ready, 0))
            stage("up01", hx_hi, hx_lo, None)
            stage("dn01", hid_hi, hid_lo, (hid_ready, NPAIR))

            norm_stat(2)
            pe.wait_ge(evac, BASE["glu"] + 2)
            for j in range(NJ):
                g5 = recs[j % 2][:].rearrange("p (q r n) -> p q r n", q=JQ, r=2)
                pe.wait_ge(sem(f"g_in{j % 2}"), 16 * (j // 2 + 1))
                if j >= 2:
                    pe.wait_ge(sem("wst_act"), j - 1)
                    pe.wait_ge(sem("wst_dve"), j - 1)
                for q in range(JQ):
                    gp = JQ * j + q
                    for e in range(2):
                        r = slice(64 * e, 64 * e + 64)
                        for ri in range(2):
                            c0 = ri * GP * GC + gp * GC
                            pe.matmul(ps[:, 6 + e, gp * GC:(gp + 1) * GC], g5[r, q, ri, :],
                                      cc[r, c0:c0 + GC], start=(ri == 0), stop=(ri == 1))
                    for ri in range(2):
                        m = 2 * q + ri
                        ins = pe.transpose(ps[:, 2 * (j % 2) + m // 4, (m % 4) * P:(m % 4) * P + P],
                                           g5[:, q, ri, :], ident[:])
                ins.then_inc(sem("resp_done"), 1)

            def states_in(j):
                pe.wait_ge(sem("v_used"), j - 1) if j >= 2 else None
                for q in range(JQ):
                    gp = JQ * j + q
                    for ri in range(2):
                        for e in range(2):
                            g = 2 * gp + e
                            c0 = (gp * 2 + ri) * P + 64 * e
                            ins = pe.matmul(ps[64 * e:64 * e + 64, 2 * (j % 2) + ri, q * 72:(q + 1) * 72],
                                            wst[:, c0:c0 + 64], u_in[:, g * UW + NS:(g + 1) * UW],
                                            start=True, stop=True)
                ins.then_inc(sem("v_done"), 1)

            def outputs(j):
                pe.wait_ge(sem(f"c_in{j % 2}"), 16 * (j // 2 + 1))
                pe.wait_ge(sem("x_done"), j + 1)
                if j == 0:
                    pe.wait_ge(sem("toep_in"), 16 * CH)
                    pe.wait_ge(sem("x_seeded"), 1)
                    pe.wait_ge(sem("rsb_done"), 1)
                if j >= 2:
                    pe.wait_ge(sem("yc_done"), j - 1)
                c5 = recs[j % 2][:].rearrange("p (q r n) -> p q r n", q=JQ, r=2)
                t3 = toep[:].rearrange("p (m g) -> p m g", g=GROUPS)
                for q in range(JQ):
                    gp = JQ * j + q
                    for e in range(2):
                        r = slice(64 * e, 64 * e + 64)
                        g = 2 * gp + e
                        out = ps[:, 4 + 2 * (j % 2) + e, q * 72:(q + 1) * 72]
                        pe.matmul(out, t3[:, :, g], u_in[:, g * UW:g * UW + 72], start=True, stop=False)
                        for ri in range(2):
                            c0 = (gp * 2 + ri) * XW
                            ins = pe.matmul(out, c5[r, q, ri, :], xst[r, c0:c0 + 72], start=False,
                                            stop=(ri == 1))
                ins.then_inc(sem("y_mm"), 1)

            pe.wait_ge(sem("wst_act"), NJ)
            pe.wait_ge(sem("wst_dve"), NJ)
            pe.wait_ge(sem("u_in"), 16 * (CH + 2))
            for j in range(NJ + 2):
                if j < NJ:
                    states_in(j)
                if j >= 2:
                    outputs(j - 2)

            stage("glu", op_hi, op_lo, (op_ready, 9))
            stage("up10", hx_hi, hx_lo, (hx_ready, 2 * KT))
            stage("dn10", hid_hi, hid_lo, (hid_ready, 2 * NPAIR))
            stage("up11", hx_hi, hx_lo, None)
            stage("dn11", hid_hi, hid_lo, (hid_ready, 3 * NPAIR))


def kernel(**inputs):
    import numpy as np
    import concourse.bacc as _bacc
    from concourse import mybir as _mybir
    from concourse.bass_utils import run_bass_kernel_spmd as _run

    a = {k: np.asarray(v) for k, v in inputs.items()}
    f = a["x_prompt"].dtype
    d = {}
    d["xT"] = np.concatenate([a["x_prompt"].reshape(SEQ, D), a["x_sample"].reshape(NS, D)]).T
    wq = a["w_qkv"][0]
    q = wq[:, :D].reshape(KT, P, 2, 2, 4, HD).transpose(2, 4, 1, 0, 3, 5).reshape(8, P, KT * P)
    kv = wq[:, D:].reshape(KT, P, 4, P).transpose(2, 1, 0, 3).reshape(4, P, KT * P)
    d["wqkv"] = np.concatenate([q, kv])
    d["wo"] = a["w_o"][0].reshape(2, 2, 4, HD, KT, P).transpose(4, 1, 3, 0, 2, 5).reshape(KT, P, KT * P)
    d["wglu"] = a["w_glu"][0].reshape(KT, P, 2, KT, P).transpose(3, 2, 1, 0, 4).reshape(2 * KT, P, KT * P)
    d["wup"] = a["w_up"].reshape(2, KT, P, 2, 2 * NPAIR, P).transpose(0, 4, 3, 2, 1, 5).reshape(-1, P, KT * P)
    d["wdn"] = a["w_down"].reshape(2, 2, NPAIR, P, KT, P).transpose(0, 1, 4, 3, 2, 5).reshape(-1, P, NPAIR * P)
    d["ones"] = np.full((P, P), 1.0 / D, f)
    d["bdiag"] = np.kron(np.eye(2), np.full((HD, HD), 1.0 / HD)).astype(f)
    d["ident"] = np.eye(P, dtype=f)
    b16 = _mybir.dt.np(_mybir.dt.bfloat16)
    d["ident16"] = np.eye(P).astype(b16)
    r, c = np.arange(P)[:, None], np.arange(P)[None, :]
    off = np.full((P, P), -1e30)
    prev, same = np.where(c > r, 0.0, off), np.where(c <= r, 0.0, off)
    d["masks"] = np.concatenate([off, same, prev, same, prev, same, prev, same], 1).astype(b16)
    g = np.stack([a["norm_mix"][0], a["norm_ffn"][0], a["norm_mix"][1], a["norm_ffn"][1]])
    d["gains"] = g.reshape(4, KT, P).transpose(2, 0, 1).reshape(P, 4 * KT)
    d["qk_gain"] = np.concatenate([np.stack([a["q_norm"][0], a["k_norm"][0]], 1)] * 2)
    d["dskip"] = a["ssm_d"][0].reshape(KT, P).T
    d["sinks"] = a["sinks"]
    d["sink_col"] = a["sinks"].reshape(HEADS, 1)
    d["cache_k"] = a["cache_k"][0].reshape(NS, P, KVH * HD)
    d["cache_v"] = a["cache_v"][0].reshape(NS, P, KVH * HD)
    d["a_re"] = a["ssm_a_re"][0].reshape(GP, P).T
    d["a_im"] = a["ssm_a_im"][0].reshape(GP, P).T
    d["log_dt"] = a["ssm_log_dt"][0].reshape(GP, 2).T
    for n in ("re", "im"):
        d["b_" + n] = a["ssm_b_" + n][0].reshape(GP, P, GC).transpose(1, 0, 2).reshape(P, GP * GC)
        d["c_" + n] = a["ssm_c_" + n][0].reshape(GP, 2, GC, ST).transpose(1, 3, 0, 2).reshape(P, GP * GC)
        d["h0_" + n] = a["state_ssm_" + n][0].reshape(NS, GP, P).transpose(2, 1, 0).reshape(P, GP * NS)
    d["conv_w"] = a["conv_w"].reshape(2, 3, 2, 22, P).transpose(0, 4, 3, 2, 1).reshape(2, P, 132)
    d["conv_b"] = a["conv_b"].reshape(2, 2, 22, P).transpose(0, 3, 2, 1).reshape(2, P, 44)
    d["conv_buf"] = a["state_conv"].reshape(2, NS, 2, 2, 22, P).transpose(0, 5, 2, 4, 3, 1).reshape(2, P, -1)
    outs = {"yT": (D, TOK), "k_prompt": (P, 2, P), "v_prompt": (P, 2, P), "k_sample": (NS, P, KVH * HD),
            "v_sample": (NS, P, KVH * HD), "x_fin": (P, 2 * GP), "xs_new": (P, 2 * GP * NS),
            "conv_rows": (2, P, 440), "conv_second": (2, P, 44 * NS)}

    nc = _bacc.Bacc("TRN2", target_bir_lowering=False, num_devices=1)
    arrays, ins, res = {}, {}, {}
    for name, v in d.items():
        v = np.ascontiguousarray(v)
        arrays[f"in_{name}"] = v
        ins[name] = nc.dram_tensor(f"in_{name}", v.shape, _mybir.dt.from_np(v.dtype), kind="ExternalInput").ap()
    for name, shape in outs.items():
        res[name] = nc.dram_tensor(f"out_{name}", shape, _mybir.dt.from_np(f), kind="ExternalOutput").ap()
    trunk_program(nc, ins, res)
    got = _run(nc, [arrays], core_ids=[0]).results[0]
    o = {name: np.asarray(got[f"out_{name}"]) for name in outs}

    y = np.ascontiguousarray(o["yT"].T)
    rows = lambda t: np.ascontiguousarray(t.transpose(2, 1, 0)).reshape(1, 1, P, KVH, HD)
    cache = lambda t: t.reshape(1, NS, P, KVH, HD)
    fin = o["x_fin"].reshape(2, ST, GP, 2).transpose(3, 2, 0, 1).reshape(2, 1, 1, GROUPS, ST)
    new = o["xs_new"].reshape(2, ST, 2, GP, NS).transpose(2, 4, 3, 0, 1).reshape(2, 1, NS, GROUPS, ST)
    cr = o["conv_rows"].reshape(2, P, 22, 2, 10).transpose(0, 4, 3, 2, 1).reshape(2, 10, F2)
    cs = o["conv_second"].reshape(2, P, 22, 2, NS).transpose(0, 4, 3, 2, 1).reshape(2, NS, F2)
    con = np.ascontiguousarray
    return (y[:SEQ].reshape(1, SEQ, D), y[SEQ:].reshape(NS, 1, D), rows(o["k_prompt"]), rows(o["v_prompt"]),
            cache(o["k_sample"]), cache(o["v_sample"]), con(fin[0]), con(fin[1]), con(new[0]), con(new[1]),
            con(cr[:, None, :2]), con(np.stack([cs, cr[:, 2:]], 2)))
```

```python
import math
from contextlib import ExitStack

import concourse.bass as bass
from concourse import mybir

ALU = mybir.AluOpType
ACT = mybir.ActivationFunctionType
AX = mybir.AxisListType
F32 = mybir.dt.float32
F32R = mybir.dt.float32r
BF16 = mybir.dt.bfloat16

P = 128
D, SEQ, NS = 1024, 512, 8
TOK = SEQ + NS
HALF = TOK // 2
KT = D // P
FF, F2 = 2816, 5632
NPAIR = FF // P // 2
HEADS, HD, KVH = 16, 64, 4
QK = (HEADS + KVH) // 2
NB = SEQ // P
GROUPS, GC, ST = 64, 16, 64
CH = 8
NC = SEQ // CH
GP = GROUPS // 2
JQ = 4
NJ = GP // JQ
EPS = 1e-6
SCALE = HD ** -0.5
UCOL = 2 + TOK
MAGIC = 12582912.0
PI = math.pi

STAGES = [("qkv", "wqkv", 0, 12, KT), ("wo", "wo", 0, 8, KT)]
for _l in range(2):
    if _l:
        STAGES.append(("glu", "wglu", 0, 16, KT))
    for _h in range(2):
        STAGES.append((f"up{_l}{_h}", "wup", (_l * 2 + _h) * 2 * NPAIR, 2 * NPAIR, KT))
        STAGES.append((f"dn{_l}{_h}", "wdn", (_l * 2 + _h) * KT, KT, NPAIR))
BASE, _u = {}, 0
for _s in STAGES:
    BASE[_s[0]] = _u
    _u += _s[3]
ORDER = [s[0] for s in STAGES]
INFO = {s[0]: s for s in STAGES}
NORM_OF = {"qkv": 0, "up00": 1, "up10": 3}
PREPARES = {"wo": 1, "dn01": 2, "glu": 3}
HX_NORM = {0: 0, 1: 1, 3: 2}




def a_split(a):
    return a // 8, (a // 2) % 4, a % 2


def a_head(a):
    p, g, e = a_split(a)
    return 8 * p + 4 * e + g


def trunk_program(nc, i, o):
    with ExitStack() as ctx:
        sems = {}

        def sem(name):
            if name not in sems:
                sems[name] = ctx.enter_context(nc.semaphore(name))
            return sems[name]

        cur = [(nc.sbuf_base + 63) // 64 * 64]

        def place(name, cols, dt=F32, at=None):
            size = (cols * (2 if dt == BF16 else 4) + 31) // 32 * 32
            off = cur[0] if at is None else at
            if at is None:
                cur[0] += size
            t = nc.alloc_sbuf_tensor_at(name, [P, cols], dt, offset=off)
            return t, off

        x, _ = place("x", KT * TOK)
        w_raw, w_hi, w_lo = [], [], []
        for b in range(2):
            w_raw.append(place(f"w_raw{b}", NPAIR * P)[0])
            w_hi.append(place(f"w_hi{b}", NPAIR * P, F32R)[0])
            w_lo.append(place(f"w_lo{b}", NPAIR * P, F32R)[0])
        hx_hi, HX = place("hx_hi", KT * TOK, F32R)
        hx_lo, _ = place("hx_lo", KT * TOK, F32R)
        hid_hi, D0 = place("hid_hi", NPAIR * TOK, F32R)
        hid_lo, _ = place("hid_lo", NPAIR * TOK, F32R)
        op_hi, _ = place("op_hi", KT * TOK, F32R, at=D0)
        op_lo, _ = place("op_lo", KT * TOK, F32R, at=D0 + 4 * KT * TOK)
        D1 = cur[0]
        XW = NC + NS + 1
        UW = NC + 2 * NS
        YW = NC + NS
        cur[0] += 4 * (GROUPS * UW + 2 * GP * XW)
        qkvT, _ = place("qkvT", 12 * TOK, at=D1)
        vtok, _ = place("vtok", NB * 256, at=D1 + 48 * TOK)
        vc, _ = place("vc", NS * 256, at=D1 + 48 * TOK + 4096)
        kc, _ = place("kc", NS * 256, at=D0 + 8 * KT * TOK)
        new_rows, _ = place("new_rows", 512, at=D0 + 8 * KT * TOK + 8192)
        probs = [place(f"probs{b}", NB * 256, at=HX + 4096 * b)[0] for b in range(2)]
        probsT = [place(f"probsT{b}", 7 * P, at=HX + 8192 + 3584 * b)[0] for b in range(2)]
        ksT, _ = place("ksT", NS * 2 * P, at=HX + 15360)
        s_st, _ = place("s_st", P, at=HX + 23552)
        s_pr, _ = place("s_pr", P, at=HX + 24064)
        s_pT, _ = place("s_pT", P, at=HX + 24576)
        qk_rms, _ = place("qk_rms", TOK, at=HX + 25088)
        up_row = [place(f"up_row{b}", UCOL, at=D1 + 2112 * b)[0] for b in range(2)]
        conv = [place(f"conv{b}", TOK, at=D1 + 4224 + 2112 * b)[0] for b in range(2)]
        silu_g, _ = place("silu_g", TOK, at=D1 + 8448)
        hid, _ = place("hid", TOK, at=D1 + 10560)
        toep, _ = place("toep", CH * GROUPS * GC, at=D0)
        recs = [place(f"recs{b}", JQ * 2 * P, at=D0 + 32768 + 4096 * b)[0] for b in range(2)]
        rots = [place(f"rots{b}", 2 * JQ * NC, at=D0 + 40960 + 2048 * b)[0] for b in range(2)]
        wst, _ = place("wst", GP * 2 * P, at=HX)
        yc = [place(f"yc{b}", CH * P, at=HX + 4 * CH * P * b)[0] for b in range(2)]
        u_in, _ = place("u_in", GROUPS * UW, at=D1)
        xst, _ = place("xst", GP * 2 * XW, at=D1 + 4 * GROUPS * UW)
        hg, _ = place("hg", KT * TOK, at=D1 + 4 * GROUPS * UW)
        z_hi, _ = place("z_hi", KT * TOK, F32R, at=D1)
        z_lo, _ = place("z_lo", KT * TOK, F32R, at=D1 + 4 * GROUPS * UW)
        glu_in = [place(f"glu_in{b}", TOK, at=D0 + 2112 * b)[0] for b in range(2)]
        glu_out, _ = place("glu_out", TOK, at=D0 + 4224)
        ones, _ = place("ones", P)
        head_mean, _ = place("head_mean", 2 * 2 * QK - 2)
        ident, _ = place("ident", P)
        ident16, _ = place("ident16", P, BF16)
        masks, _ = place("masks", 1024, BF16)
        gains, _ = place("gains", 4 * KT)
        qk_gain, _ = place("qk_gain", 2)
        dskip, _ = place("dskip", GROUPS)
        step_sel, _ = place("step_sel", CH)
        rstd_u, _ = place("rstd_u", UW)
        sink, _ = place("sink", HEADS)
        nsink, _ = place("nsink", HEADS)
        sink_row, _ = place("sink_row", 1)
        nsink_row, _ = place("nsink_row", 1)
        eps, _ = place("eps", 1)
        soft, _ = place("soft", 2 * 16)
        s_soft, _ = place("s_soft", 8)
        sq = [place(f"sq{b}", TOK)[0] for b in range(2)]
        sqs, _ = place("sqs", TOK)
        rstd, _ = place("rstd", TOK)
        cw, _ = place("cw", 44 * 3)
        cb, _ = place("cb", 44)
        cbuf, _ = place("cbuf", 2 * 44 * NS)
        pre, _ = place("pre", 44 * NS)
        crow, _ = place("crow", 44 * 10)
        h0, _ = place("h0", 2 * GP * NS)
        ah0, _ = place("ah0", 2 * GP * NS)
        x_fin, _ = place("x_fin", 2 * GP)
        mag8, _ = place("mag8", GP)
        rec, REC = place("rec", JQ * 2 * P)
        ptmp, _ = place("ptmp", 2 * JQ * 64)
        bb, BB = place("bb", 2 * GP * GC)
        cc, CC = place("cc", 2 * GP * GC)
        NL = 9
        pw, _ = place("pw", NL * 2 * 2 * GP)
        ccd, _ = place("ccd", 4 * JQ * 2 * 2 * GC, at=BB)
        rsb = [sq[1], sqs]
        skip_d, _ = place("skip_d", GROUPS * GC, at=REC)
        vrot = [place(f"vrot{b}", JQ * NC, at=REC + 1024 * b)[0] for b in range(2)]
        vtmp = [place(f"vtmp{b}", JQ * NC, at=REC + 2048 + 1024 * b)[0] for b in range(2)]
        zst = [place(f"zst{b}", 2 * JQ * NC, at=CC + 2048 * b)[0] for b in range(2)]
        head_rows, _ = place("head_rows", QK * P, at=D0 + 16384)
        prm, _ = place("prm", 16 * GP, at=D0 + 8192)
        braw, _ = place("braw", 2 * GP * GC, at=D0)
        btmp, _ = place("btmp", 2 * GP * GC, at=D0 + 4096)
        assert cur[0] <= nc.sbuf_usable_end, (cur[0], nc.sbuf_usable_end)

        ps = ctx.enter_context(nc.psum_tensor("ps", [P, 8, 512], F32))

        def scratch(name, shape):
            return nc.dram_tensor(name, shape, F32).ap()

        g_scr = scratch("g_scr", (NJ, P, JQ * 2 * P))
        c_scr = scratch("c_scr", (NJ, P, JQ * 2 * P))
        e_scr = scratch("e_scr", (NJ, P, 2 * JQ * NC))
        h_scr = scratch("h_scr", (D, TOK))

        def tiles(t, k, n=1, w=TOK):
            return t[:, bass.ds(k * w, n * w)]

        def halves(ap):
            return ap.rearrange("p (h n) -> p h n", h=2)

        def acc(u):
            return ps[:, 2 * u:2 * u + 2, 0:HALF]

        misc = [ps[:, 4:6, 0:HALF], ps[:, 6:8, 0:HALF]]

        w_in = [sem("w_in0"), sem("w_in1")]
        hi_done, lo_done = sem("w_hi_done"), sem("w_lo_done")
        units_done, evac = sem("units_done"), sem("evac")
        sq_done, sqs_done = sem("sq_done"), sem("sqs_done")
        hx_hi_done, hx_ready = sem("hx_hi_done"), sem("hx_ready")
        stat_done, sd_done, rstd_done = sem("stat_done"), sem("sd_done"), sem("rstd_done")
        op_ready, hid_ready = sem("op_ready"), sem("hid_ready")
        consts_in, prm_in, cache_in, conv_in = (sem(n) for n in (
            "consts_in", "prm_in", "cache_in", "conv_in"))
        conv_first, conv_done, conv_part = sem("conv_first"), sem("conv_done"), sem("conv_part")
        silu_done, hid_prod, hid_hi_done = sem("silu_done"), sem("hid_prod"), sem("hid_hi_done")
        crow_done, crow_out = sem("crow_done"), sem("crow_out")
        out_done = sem("out_done")
        n_out = [0]

        def loop(eng, n, first, body):
            for k in range(first):
                body(k)
            with eng.Fori(first, n) as k:
                body(k)

        def ccd_view(j):
            n = JQ * 2 * 2 * GC
            return ccd[:, (j % 4) * n:(j % 4 + 1) * n].rearrange("p (q r e c) -> p q r e c", q=JQ, r=2, e=2)

        def by_step(ap):
            return ap.rearrange("p (c s) -> p s c", s=CH)

        turned = ps[:, 6:8, 0:4 * YW].rearrange("p b (s n) -> p b s n", n=YW)[:, :, :, NS:YW]

        block = ctx.enter_context(nc.Block())

        @block.sync
        def _(sp):
            def load_unit(stage, n):
                name, w, row, _, kt = INFO[stage]
                for b in range(2):
                    u = BASE[stage] + 2 * n + b
                    sp.wait_ge(lo_done, u + 1)
                    src = i[w][bass.ds(row + 2 * n + b, 1)].rearrange("o p c -> (o p) c")
                    sp.dma_start(w_raw[b][:, 0:kt * P], src).then_inc(w_in[b], 16)

            def load_stage(stage, first=0):
                with sp.Fori(first, INFO[stage][3] // 2) as n:
                    load_unit(stage, n)

            def store(dst, src):
                sp.dma_start(dst, src).then_inc(out_done, 16)
                n_out[0] += 16

            sp.dma_start(gains[:], i["gains"]).then_inc(sem("gains_in"), 16)
            for k in range(0, KT, 2):
                sp.dma_start(x[:, k * TOK:(k + 2) * TOK].rearrange("p (k t) -> p k t", k=2),
                             i["xT"][k * P:(k + 2) * P, :].rearrange("(k p) t -> p k t", p=P)
                             ).then_inc(sem(f"x_in{k}"), 16)
            load_unit("qkv", 0)
            for t, name in ((ones, "ones"), (head_mean, "head_mean"), (ident, "ident"), (ident16, "ident16"),
                            (masks, "masks"), (qk_gain, "qk_gain"), (dskip, "dskip"),
                            (step_sel, "step_sel")):
                sp.dma_start(t[:], i[name]).then_inc(consts_in, 16)
            sp.dma_start(head_rows[0:2 * QK, :], i["head_rows"]).then_inc(consts_in, 16)
            sp.dma_start(sink[:], i["sinks"].to_broadcast([P, HEADS])).then_inc(consts_in, 16)
            for n in range(NS):
                sp.dma_start(sink_row[n * HEADS:(n + 1) * HEADS, :], i["sink_col"]).then_inc(consts_in, 16)
            for n, name in enumerate(("a_re", "a_im")):
                sp.dma_start(prm[:, n * GP:(n + 1) * GP], i[name]).then_inc(prm_in, 16)
            for e in range(2):
                sp.dma_start(prm[64 * e:64 * e + 64, 2 * GP:3 * GP],
                             i["log_dt"][e:e + 1, :].to_broadcast([64, GP])).then_inc(prm_in, 16)
            for n, name in enumerate(("b_re", "b_im")):
                sp.dma_start(braw[:, n * GP * GC:(n + 1) * GP * GC], i[name]).then_inc(prm_in, 16)
            for n, name in enumerate(("c_re", "c_im")):
                sp.dma_start(cc[:, n * GP * GC:(n + 1) * GP * GC], i[name]).then_inc(prm_in, 16)
            for n, name in enumerate(("h0_re", "h0_im")):
                sp.dma_start(h0[:, n * GP * NS:(n + 1) * GP * NS], i[name]).then_inc(prm_in, 16)
            load_unit("qkv", 1)
            for t, name in ((cw, "conv_w"), (cb, "conv_b"), (cbuf, "conv_buf")):
                sp.dma_start(t[:], i[name][0]).then_inc(conv_in, 16)
            sp.dma_start(vc[0:P - 1, :].rearrange("t (n c) -> t n c", n=NS),
                         i["cache_v"][:, 1:P, :].rearrange("n t c -> t n c")).then_inc(cache_in, 16)
            store(o["k_sample"][:, 0:P - 1, :], i["cache_k"][:, 1:P, :])
            store(o["v_sample"][:, 0:P - 1, :], i["cache_v"][:, 1:P, :])
            load_stage("qkv", 2)
            load_unit("wo", 0)
            sp.dma_start(kc[0:P - 1, :].rearrange("t (n c) -> t n c", n=NS),
                         i["cache_k"][:, 1:P, :].rearrange("n t c -> t n c")).then_inc(sem("kc_in"), 16)
            sp.wait_ge(sem("new_rows_done"), 1)
            for n in range(NS):
                sp.dma_start(vc[P - 1:P, n * 256:(n + 1) * 256],
                             new_rows[n:n + 1, 0:256]).then_inc(sem("vc_new"), 16)
            store(o["v_sample"][:, P - 1, :], new_rows[0:NS, 0:256])
            store(o["k_sample"][:, P - 1, :], new_rows[0:NS, 256:512])
            sp.wait_ge(sem("qk_normed"), 10)
            store(o["k_prompt"], tiles(qkvT, 8, 2).rearrange("p (k t) -> p k t", k=2)[:, :, SEQ - P:SEQ])
            store(o["v_prompt"], tiles(qkvT, 10, 2).rearrange("p (k t) -> p k t", k=2)[:, :, SEQ - P:SEQ])
            sp.wait_ge(out_done, n_out[0])
            sp.sem_inc(sem("attn_stored"), 1)
            load_stage("wo", 1)
            for s in ("up00", "dn00", "up01"):
                load_stage(s)

            def conv_out(layer):
                sp.wait_ge(crow_done, 44 * (layer + 1))
                store(o["conv_rows"][layer], crow[:])
                store(o["conv_second"][layer], cbuf[:, 44 * NS:2 * 44 * NS])

            sp.wait_ge(sem("scr_out"), 16 * 3 * NJ)
            u3 = u_in[:].rearrange("p (g c) -> p g c", g=GROUPS)
            h3 = h_scr.rearrange("(g c) t -> c g t", c=GC)

            def u_tile(k):
                sp.wait_ge(sem(f"h_out{k % 2}"), 16 * (k // 2 + 1))
                g = slice(CH * k, CH * (k + 1))
                for s in range(CH):
                    sp.dma_start(u3[GC * s:GC * (s + 1), g, NS:NS + NC],
                                 h3[:, g, s * NC:(s + 1) * NC]).then_inc(sem("u_in"), 16)
                sp.dma_start(u3[0:GC, g, 0:NS], h3[:, g, SEQ:TOK]).then_inc(sem("u_in"), 16)
                sp.dma_start(u3[P - GC:P, g, NS + NC:UW], h3[:, g, SEQ:TOK]).then_inc(sem("u_in"), 16)

            load_unit("dn01", 0)
            load_unit("dn01", 1)
            sp.wait_ge(units_done, BASE["dn01"] + 2)
            for j in range(NJ):
                sp.dma_start(wst[:, j * 1024:(j + 1) * 1024], g_scr[j]).then_inc(sem("g_in"), 16)
            sp.wait_ge(sem("u_zeroed"), 1)
            for k in range(KT):
                if k % 2 == 0:
                    load_unit(*(("dn01", 2 + k // 2) if k < 4 else ("glu", k // 2 - 2)))
                sp.wait_ge(sem("h_done"), k + 1)
                sp.dma_start(h_scr[k * P:(k + 1) * P, :], tiles(hg, k)).then_inc(sem(f"h_out{k % 2}"), 16)
                if k >= 1:
                    u_tile(k - 1)
            def load_step(j):
                if j >= 2:
                    sp.wait_ge(sem("x_done"), j - 1)
                sp.dma_start(rots[j % 2][:], e_scr[j]).then_inc(sem(f"e_in{j % 2}"), 16)
                if j >= 2:
                    sp.wait_ge(sem("y_mm"), j - 1)
                sp.dma_start(recs[j % 2][:], c_scr[j]).then_inc(sem(f"c_in{j % 2}"), 16)

            u_tile(KT - 1)
            sp.wait_ge(units_done, BASE["glu"] + 2)
            load_step(0)
            load_step(1)
            for h in range(2):
                sp.wait_ge(sem("rsb_full"), h + 1)
                sp.wait_ge(sem("toep_zeroed"), h + 1)
                for t in range(CH):
                    n, c = GC * (t + 1), CH * h + t
                    sp.dma_start(toep[0:n, c * 512:(c + 1) * 512],
                                 rsb[h][P - n:P, 0:512]).then_inc(sem(f"toep_in{h}"), 16)
            for j in range(2, NJ):
                load_step(j)
            conv_out(0)
            sp.wait_ge(sem("x_fin_done"), NJ)
            sp.wait_ge(sem("v_used"), NJ)
            store(o["x_fin"], x_fin[:])
            store(o["xs_new"], ah0[:])
            sp.wait_ge(out_done, n_out[0])
            sp.sem_inc(crow_out, 1)
            for t, name in ((cw, "conv_w"), (cb, "conv_b"), (cbuf, "conv_buf")):
                sp.dma_start(t[:], i[name][1]).then_inc(conv_in, 16)

            load_stage("glu", 2)
            for s in ("up10", "dn10", "up11", "dn11"):
                load_stage(s)
            conv_out(1)
            for m in range(KT):
                sp.wait_ge(evac, BASE["dn11"] + m + 3)
                store(o["yT"][m * P:(m + 1) * P, :], tiles(x, m))
            sp.wait_ge(out_done, n_out[0])

        @block.gpsimd
        def _(pool):
            pl = sem("pool_step")
            done = [0]

            def after(ins, j=None):
                done[0] += 1
                ins.then_inc(pl, 1)
                pool.wait_ge(pl, done[0] if j is None else j * per[0] + done[0])

            per = [0]

            def pre_rows():
                w3 = cw[:].rearrange("p (t j) -> p t j", j=3)
                c3 = cbuf[:].rearrange("p (r t n) -> p r t n", r=2, n=NS)
                p3 = pre[:].rearrange("p (t n) -> p t n", n=NS)
                for r, out in ((0, c3[:, 0]), (1, p3)):
                    after(pool.tensor_tensor(out, c3[:, r], w3[:, :, r:r + 1].to_broadcast([P, 44, NS]),
                                             ALU.mult))
                after(pool.tensor_tensor(p3, p3, c3[:, 0], ALU.add))
                pool.sem_inc(sem("pre_done"), 1)

            pool.wait_ge(conv_in, 48)
            pre_rows()
            pool.wait_ge(sem("bb_done"), 1)
            start = done[0]
            done[0] = 0

            def cmul(j, o_re, o_im, a_re, a_im, b_re, b_im, n, conj=False):
                t0 = ptmp[:, 0:JQ * n].rearrange("p (q n) -> p q n", q=JQ)
                t1 = ptmp[:, JQ * 64:JQ * (64 + n)].rearrange("p (q n) -> p q n", q=JQ)
                tt = pool.tensor_tensor
                after(tt(t0, a_re, b_re, ALU.mult), j)
                after(tt(t1, a_im, b_im, ALU.mult), j)
                after(tt(o_re, t0, t1, ALU.add if conj else ALU.subtract), j)
                after(tt(t0, a_im, b_re, ALU.mult), j)
                after(tt(t1, a_re, b_im, ALU.mult), j)
                after(tt(o_im, t0, t1, ALU.subtract if conj else ALU.add), j)

            def power(level, kind, j, n):
                res = []
                for ri in range(2):
                    at = ((level * 2 + ri) * 2 + kind) * GP
                    res.append(pw[:, bass.ds(at + j * JQ, JQ)].rearrange("p (q o) -> p q o", o=1)
                               .to_broadcast([P, JQ, n]))
                return res

            def tables(j):
                done[0] = start
                base_step = 0
                r5 = rec[:].rearrange("p (q r s c) -> p q r s c", q=JQ, r=2, s=CH)
                r4 = rec[:].rearrange("p (q r n) -> p q r n", q=JQ, r=2)

                def seed(src, s):
                    for ri in range(2):
                        v = src[:, bass.ds(ri * GP * GC + j * JQ * GC, JQ * GC)].rearrange(
                            "p (q c) -> p q c", q=JQ)
                        after(pool.tensor_copy(r5[:, :, ri, s, :], v), j)

                def blk(ri, s, n):
                    return r4[:, :, ri, s * GC:(s + n) * GC]

                seed(bb, CH - 1)
                for lev, dst, src, n in ((0, 6, 7, 1), (1, 4, 6, 2), (2, 0, 4, 4)):
                    pr, pi = power(lev, 0, j, n * GC)
                    cmul(j, blk(0, dst, n), blk(1, dst, n), blk(0, src, n), blk(1, src, n), pr, pi, n * GC)
                pool.dma_start(g_scr[bass.ds(j, 1)].rearrange("o p c -> (o p) c"), rec[:]).then_inc(scr, 16)
                pool.wait_ge(scr, 48 * j + 16)
                seed(cc, 0)
                pr, pi = power(0, 0, j, GC)
                cmul(j, blk(0, 1, 1), blk(1, 1, 1), blk(0, 0, 1), blk(1, 0, 1), pr, pi, GC, True)
                for ri in range(2):
                    after(pool.tensor_copy(r5[:, :, ri, 0, :], r5[:, :, ri, 1, :]), j)
                for lev, dst, src, n in ((0, 1, 0, 1), (1, 2, 0, 2), (2, 4, 0, 4)):
                    pr, pi = power(lev, 0, j, n * GC)
                    cmul(j, blk(0, dst, n), blk(1, dst, n), blk(0, src, n), blk(1, src, n), pr, pi,
                         n * GC, True)
                pool.dma_start(c_scr[bass.ds(j, 1)].rearrange("o p c -> (o p) c"), rec[:]).then_inc(scr, 16)
                pool.wait_ge(scr, 48 * j + 32)
                e4 = rec[:, 0:2 * JQ * NC].rearrange("p (r q c) -> p r q c", r=2, q=JQ)
                for ri, v in enumerate(power(3, 1, j, 1)):
                    after(pool.tensor_copy(e4[:, ri, :, 0:1], v), j)
                for lev in range(6):
                    n = 1 << lev
                    pr, pi = power(3 + lev, 1, j, n)
                    cmul(j, e4[:, 0, :, n:2 * n], e4[:, 1, :, n:2 * n], e4[:, 0, :, 0:n],
                         e4[:, 1, :, 0:n], pr, pi, n)
                pool.dma_start(e_scr[bass.ds(j, 1)].rearrange("o p c -> (o p) c"),
                               rec[:, 0:2 * JQ * NC]).then_inc(scr, 16)
                pool.wait_ge(scr, 48 * j + 48)
                assert done[0] - start == per[0], done[0] - start

            scr = sem("scr_out")
            per[0] = 2 * 4 + 6 * (3 + 1 + 3 + 6)
            for j in range(NJ):
                tables(j)
            done[0] = start + NJ * per[0]

            def block_diagonals(j):
                d = ccd_view(j)
                if j >= 4:
                    pool.wait_ge(sem("resp_done"), j - 3)
                c4 = cc[:].rearrange("p (r q c) -> p q r c", r=2, q=GP)
                for e in range(2):
                    r = slice(64 * e, 64 * e + 64)
                    after(pool.tensor_copy(d[r, :, :, e, :], c4[r, JQ * j:JQ * (j + 1)]))
                pool.sem_inc(sem("ccd_done"), 1)

            after(pool.memset(ccd[:], 0.0))
            for j in range(4):
                block_diagonals(j)
            pool.wait_ge(hid_ready, 2 * NPAIR)
            pool.wait_ge(crow_done, 44)
            u3 = u_in[:].rearrange("p (g c) -> p g c", g=GROUPS)
            pool.memset(u3[:, :, 0:NS], 0.0)
            pool.memset(u3[:, :, NS + NC:UW], 0.0).then_inc(sem("u_zeroed"), 1)
            pool.wait_ge(units_done, BASE["glu"] + 2)
            for h in range(2):
                pool.memset(toep[:, h * CH * 512:(h + 1) * CH * 512], 0.0).then_inc(sem("toep_zeroed"), 1)
                for j in (4 + 2 * h, 5 + 2 * h):
                    block_diagonals(j)
            x4 = xst[:].rearrange("p (q r c) -> p q r c", q=GP, r=2)
            for b in range(2):
                pool.wait_ge(sem(f"h_out{b}"), 8 * KT)
            pool.memset(x4[:, :, :, NS:NS + 1], 0.0)
            h4 = h0[:].rearrange("p (r q n) -> p r q n", r=2, q=GP)
            for ri in range(2):
                ins = pool.tensor_copy(x4[:, :, ri, 0:NS], h4[:, ri])
            ins.then_inc(sem("x_seeded"), 1)
            f3 = x_fin[:].rearrange("p (q r) -> p q r", r=2)
            for j in range(NJ):
                z = zst[j % 2][:].rearrange("p (r q c) -> p r q c", r=2, q=JQ)
                e = rots[j % 2][:].rearrange("p (r q c) -> p r q c", r=2, q=JQ)
                t0 = ptmp[:, 0:JQ * 64].rearrange("p (q c) -> p q c", q=JQ)
                t1 = ptmp[:, JQ * 64:JQ * 128].rearrange("p (q c) -> p q c", q=JQ)
                out = x4[:, JQ * j:JQ * (j + 1), :, NS + 1:NS + 1 + NC]
                pool.wait_ge(sem("z_done"), j + 1)
                tt = pool.tensor_tensor
                tt(t0, z[:, 0], e[:, 0], ALU.mult)
                after(tt(t1, z[:, 1], e[:, 1], ALU.mult))
                after(tt(out[:, :, 0, :], t0, t1, ALU.subtract))
                tt(t0, z[:, 1], e[:, 0], ALU.mult)
                after(tt(t1, z[:, 0], e[:, 1], ALU.mult))
                tt(out[:, :, 1, :], t0, t1, ALU.add).then_inc(sem("x_done"), 1)
                pool.wait_ge(sem("x_done"), j + 1)
                pool.tensor_copy(f3[:, JQ * j:JQ * (j + 1)].rearrange("p q (r o) -> p q r o", o=1),
                                 x4[:, JQ * j:JQ * (j + 1), :, XW - 1:XW]).then_inc(sem("x_fin_done"), 1)
            pool.wait_ge(conv_in, 96)
            pre_rows()

        @block.scalar
        def _(act):
            def split(u, b, kt):
                act.wait_ge(w_in[b], 8 * (u - b) + 16)
                act.wait_ge(units_done, u + 1)
                act.activation(w_hi[b][:, 0:kt * P], w_raw[b][:, 0:kt * P], ACT.Copy).then_inc(hi_done, 1)

            def norm_in(n, k, b, slots=2):
                if not (n == 0 and isinstance(k, int) and k < 2):
                    act.wait_ge(sqs_done, n * KT + k + 1 - slots)
                act.activation(sq[b][:], tiles(x, k), ACT.Square).then_inc(sq_done, 1)
                if n in HX_NORM:
                    act.activation(tiles(hx_hi, k), tiles(x, k), ACT.Copy,
                                   scale=gains[:, bass.ds(n * KT + k, 1)]).then_inc(hx_hi_done, 1)
                if n == 2:
                    g = gains[:, bass.ds(n * KT + k, 1)]
                    act.activation(hg[:, bass.ds(k * TOK, SEQ)].rearrange("p (s c) -> p s c", s=CH),
                                   by_step(x[:, bass.ds(k * TOK, SEQ)]), ACT.Copy, scale=g)
                    act.activation(hg[:, bass.ds(k * TOK + SEQ, NS)], x[:, bass.ds(k * TOK + SEQ, NS)],
                                   ACT.Copy, scale=g).then_inc(sem("h_done"), 1)

            def norm_sd(n):
                act.wait_ge(stat_done, n + 1)
                act.activation(halves(sq[0][:]), misc[0], ACT.Sqrt, bias=eps[:]).then_inc(sd_done, 1)

            def stage(name, work, last_k=None):
                n = INFO[name][3] // 2
                kt = INFO[name][4]
                nxt = ORDER.index(name) + 1
                k_next = STAGES[nxt][4] if nxt < len(STAGES) else None

                def body(it, k):
                    for b in range(2):
                        u = BASE[name] + 2 * it + b
                        waits_norm = name in NORM_OF and isinstance(it, int) and it == 0 and b == 0
                        if waits_norm and name == "qkv":
                            norm_sd(0)
                        if k:
                            split(u + 2, b, k)
                        if waits_norm and name != "qkv":
                            norm_sd(NORM_OF[name])
                        work(it, b, u)

                first = n - 1 if name == "qkv" else 1 if name[:2] == "up" else 0
                for it in range(first):
                    body(it, kt)
                if first < n - 1:
                    with act.Fori(first, n - 1) as it:
                        body(it, kt)
                body(n - 1, k_next)

            act.wait_ge(sem("gains_in"), 16)
            act.wait_ge(sem("eps_set"), 1)
            for k in range(KT):
                act.wait_ge(sem(f"x_in{k // 2 * 2}"), 16)
                norm_in(0, k, k % 2)
            split(0, 0, KT)
            split(1, 1, KT)

            pk = [prm[:, n * GP:(n + 1) * GP] for n in range(16)]

            def prepare(it, b, u):
                if u == 1:
                    act.wait_ge(prm_in, 16 * 10)
                    act.activation(pk[2], pk[2], ACT.Exp).then_inc(sem("prm_act"), 1)
                elif u == 3:
                    act.wait_ge(sem("prm_dve"), 1)
                    act.activation(pk[3], pk[3], ACT.Exp).then_inc(sem("prm_act"), 1)
                    act.wait_ge(sem("prm_dve"), 2)
                    act.activation(prm[:, 5 * GP:7 * GP], prm[:, 5 * GP:7 * GP],
                                   ACT.Sin).then_inc(sem("prm_act"), 1)

            stage("qkv", prepare)
            act.wait_ge(consts_in, 16 * 18)

            for t in range(QK):
                act.wait_ge(evac, BASE["qkv"] + t + 3)
                if t >= 2:
                    act.wait_ge(sem("qk_summed"), t - 1)
                act.activation(sq[t % 2][:], tiles(qkvT, t), ACT.Square).then_inc(sem("qk_sq"), 1)
            act.wait_ge(sem("qk_summed"), QK)
            act.activation(halves(qk_rms[0:2 * QK, :]), ps[0:2 * QK, 4:6, 0:HALF], ACT.Sqrt,
                           bias=eps[0:2 * QK, :]).then_inc(sem("qk_sd"), 1)
            act.wait_ge(sem("v_turned"), 1)
            act.activation(vtok[:].rearrange("p (b c) -> p b c", b=2), ps[:, 0:2, :],
                           ACT.Copy).then_inc(sem("vtok_done"), 1)
            act.wait_ge(sem("ks_turned"), 1)
            act.activation(ksT[:].rearrange("p (b t) -> p b t", t=P)[:, :, 0:P - 1],
                           ps[:, 4:8, :].rearrange("p b (m t) -> p (b m) t", t=P)[:, :, 0:P - 1],
                           ACT.Copy).then_inc(sem("ksT_done"), 1)
            def attn_exp(a):
                b = a % 2
                act.wait_ge(sem("maxed"), a + 1)
                if a >= 2:
                    act.wait_ge(sem("p_turned"), a - 1)
                for blk in range(NB):
                    lo = P if blk == 0 else 0
                    act.activation(probs[b][:, blk * 256 + lo:(blk + 1) * 256],
                                   ps[:, 2 * b + blk // 2, (blk % 2) * 256 + lo:(blk % 2) * 256 + 256],
                                   ACT.Exp, bias=soft[:, 16 * b + 4 + blk:16 * b + 5 + blk], scale=SCALE,
                                   accum_out=soft[:, 16 * b + 8 + blk:16 * b + 9 + blk])
                act.activation(soft[:, 16 * b + 12:16 * b + 16], soft[:, 16 * b + 4:16 * b + 8], ACT.Exp,
                               bias=sink[:, a_head(a):a_head(a) + 1]).then_inc(sem("exp_done"), 1)

            act.wait_ge(sem("s_scored"), 1)
            act.activation(s_st[:].rearrange("p (m e g) -> p e m g", e=2, g=4),
                           ps[:, 4:6, 0:64].rearrange("p e (m g) -> p e m g", g=4),
                           ACT.Copy).then_inc(sem("s_st_done"), 1)
            attn_exp(0)
            act.wait_ge(sem("s_maxed"), 1)
            act.activation(s_pr[:], ps[:, 6, 0:P], ACT.Exp, bias=s_soft[:, 1:2], scale=SCALE,
                           accum_out=s_soft[:, 2:3])
            act.activation(s_soft[:, 3:4], s_soft[:, 1:2], ACT.Exp, bias=sink_row[:]).then_inc(sem("s_exp"), 1)
            attn_exp(1)
            act.wait_ge(sem("s_pturned"), 1)
            act.activation(s_pT[:], ps[:, 7, 0:P], ACT.Copy).then_inc(sem("s_pT_done"), 1)
            act.wait_ge(sem("s_out"), 1)
            act.activation(op_hi[:].rearrange("p (k t) -> p k t", k=KT)[:, :, SEQ:TOK],
                           ps[:, 5, 0:NS * KT].rearrange("p (n k) -> p k n", n=NS),
                           ACT.Copy).then_inc(sem("o_hi"), 1)

            def attn_turn(a):
                act.wait_ge(sem("p_turned"), a + 1)
                if a >= 2:
                    act.wait_ge(sem("pv_done"), a - 1)
                act.activation(probsT[a % 2][:, 0:512], ps[:, 4, :], ACT.Copy).then_inc(sem("pT_act"), 1)

            def attn_out(a):
                if a % 2:
                    act.wait_ge(sem("pv_done"), a + 1)
                    act.activation(tiles(op_hi, a // 2)[:, 0:SEQ], ps[:, 6 + (a // 2) % 2, :],
                                   ACT.Copy).then_inc(sem("o_hi"), 1)

            for a in range(HEADS):
                attn_turn(a)
                if a >= 1:
                    attn_out(a - 1)
                if a + 2 < HEADS:
                    attn_exp(a + 2)
            attn_out(HEADS - 1)

            def residual(n):
                def work(it, b, u):
                    act.wait_ge(evac, u + 3)
                    norm_in(n, 2 * it + b, b)
                return work

            def ffn(layer, half):
                tb = 44 * layer
                hb = (2 * layer + half) * NPAIR

                def hid_hi_of(it):
                    act.wait_ge(hid_prod, hb + it + 1)
                    act.activation(tiles(hid_hi, it), hid[:], ACT.Copy).then_inc(hid_hi_done, 1)

                def up(it, b, u):
                    t = 2 * it + b + 22 * half
                    act.wait_ge(evac, u + 3)
                    act.activation(crow[:, bass.ds(t * 10, 10)], up_row[b][:, UCOL - 10:UCOL],
                                   ACT.Copy).then_inc(crow_done, 1)
                    if not (hb == 0 and isinstance(it, int) and it == 0):
                        act.wait_ge(hid_prod, hb + it)
                    act.activation(conv[b][:], up_row[b][:, 2:UCOL], ACT.Identity,
                                   scale=cw[:, bass.ds(t * 3 + 2, 1)],
                                   bias=cb[:, bass.ds(t, 1)]).then_inc(conv_first, 1)
                    if b == 0:
                        if not isinstance(it, int) or it > 0:
                            hid_hi_of(it - 1)
                        act.wait_ge(conv_done, 2 * (hb + it) + 1)
                        if not (hb == 0 and isinstance(it, int) and it == 0):
                            act.wait_ge(hid_prod, hb + it)
                        act.activation(silu_g[:], conv[0][:], ACT.Silu).then_inc(silu_done, 1)

                if layer == 0 and half == 0:
                    act.wait_ge(sem("attn_stored"), 1)
                if layer == 1 and half == 0:
                    act.wait_ge(crow_out, 1)
                    act.wait_ge(conv_in, 96)
                stage(f"up{layer}{half}", up)
                hid_hi_of(NPAIR - 1)
                stage(f"dn{layer}{half}", residual(2) if (layer, half) == (0, 1) else (lambda it, b, u: None))

            stage("wo", residual(1))
            ffn(0, 0)
            ffn(0, 1)

            norm_sd(2)
            for j in range(NJ):
                act.wait_ge(sem("resp_done"), j + 1)
                act.activation(wst[:, j * 1024:j * 1024 + 512], ps[:, 2 * (j % 2), :],
                               ACT.Copy).then_inc(sem("wst_act"), 1)
                if j % 4 == 3:
                    h = j // 4
                    act.activation(rsb[h][:, 0:512], ps[:, 6 + h, :], ACT.Copy).then_inc(sem("rsb_done"), 1)

            for j in range(NJ + 1):
                if j >= 1:
                    c0 = (j - 1) * TOK
                    act.wait_ge(sem("z_turned"), j)
                    act.activation(z_hi[:, c0:c0 + SEQ].rearrange("p (c b s) -> p b s c", b=2, s=CH // 2),
                                   turned, ACT.Copy)
                    act.activation(z_hi[:, c0 + SEQ:c0 + TOK], ps[:, 6, 0:NS], ACT.Copy).then_inc(sem("z_hi"), 1)
                if j == NJ:
                    break
                act.wait_ge(sem("y_mm"), j + 1)
                if j >= 2:
                    act.wait_ge(sem("z_turned"), j - 1)
                for e in range(2):
                    ins = act.activation(
                        yc[j % 2][0:YW, :].rearrange("n (t q f c) -> n q t f c", t=CH, q=JQ, f=2)[:, :, :, e, :],
                        ps[0:YW, 4 + e, :].rearrange("n (q t c) -> n q t c", q=JQ, t=CH),
                        ACT.Gelu_apprx_tanh)
                ins.then_inc(sem("yc_done"), 1)

            def glu(it, b, u):
                if b == 1:
                    act.wait_ge(units_done, u + 3)
                    act.wait_ge(evac, u + 2)
                    act.activation(halves(glu_in[1][:]), acc(1), ACT.Tanh, scale=0.5).then_inc(sem("tanh_done"), 1)
                    act.wait_ge(sem("glu_done"), it + 1)
                    norm_in(3, it, 0, slots=1)

            stage("glu", glu)
            ffn(1, 0)
            ffn(1, 1)

        @block.vector
        def _(dve):
            dv = sem("dve_step")
            done = [0]

            def after(ins):
                done[0] += 1
                ins.then_inc(dv, 1)
                dve.wait_ge(dv, done[0])

            def split(u, b, kt):
                dve.wait_ge(hi_done, u + 1)
                dve.tensor_tensor(w_lo[b][:, 0:kt * P], w_raw[b][:, 0:kt * P],
                                  w_hi[b][:, 0:kt * P].bitcast(F32), ALU.subtract).then_inc(lo_done, 1)

            def norm_in(n, k, b, first=False):
                dve.wait_ge(sq_done, n * KT + k + 1)
                if first:
                    dve.tensor_copy(sqs[:], sq[b][:]).then_inc(sqs_done, 1)
                else:
                    dve.wait_ge(sqs_done, n * KT + k)
                    dve.tensor_tensor(sqs[:], sqs[:], sq[b][:], ALU.add).then_inc(sqs_done, 1)
                if n in HX_NORM:
                    dve.wait_ge(hx_hi_done, HX_NORM[n] * KT + k + 1)
                    dve.scalar_tensor_tensor(tiles(hx_lo, k), tiles(x, k), gains[:, bass.ds(n * KT + k, 1)],
                                             tiles(hx_hi, k).bitcast(F32), ALU.mult,
                                             ALU.subtract).then_inc(hx_ready, 1)

            def norm_rstd(n):
                dve.wait_ge(sd_done, n + 1)
                dve.reciprocal(rstd[:], sq[0][:]).then_inc(rstd_done, 1)
                dve.wait_ge(rstd_done, n + 1)

            def stage(name, take, work=None):
                n = INFO[name][3] // 2
                kt = INFO[name][4]
                nxt = ORDER.index(name) + 1
                k_next = STAGES[nxt][4] if nxt < len(STAGES) else None

                def body(it, k):
                    for b in range(2):
                        u = BASE[name] + 2 * it + b
                        waits_norm = name in NORM_OF and isinstance(it, int) and it == 0 and b == 0
                        if waits_norm:
                            if name != "qkv":
                                split(u + 2, b, k)
                            norm_rstd(NORM_OF[name])
                        if take:
                            take(it, b, u)
                        if k and (not waits_norm or name == "qkv"):
                            split(u + 2, b, k)
                        if work:
                            work(it, b, u)

                first = n - 1 if name == "qkv" else 1 if name[:2] == "up" or name in PREPARES else 0
                for it in range(first):
                    body(it, kt)
                if first < n - 1:
                    with dve.Fori(first, n - 1) as it:
                        body(it, kt)
                body(n - 1, k_next)

            dve.memset(eps[:], EPS).then_inc(sem("eps_set"), 1)
            dve.sem_inc(lo_done, 2)
            dve.sem_inc(evac, 2)
            after(dve.memset(soft[:], 0.0))
            dve.wait_ge(sem("gains_in"), 16)
            for k in range(KT):
                dve.wait_ge(sem(f"x_in{k // 2 * 2}"), 16)
                norm_in(0, k, k % 2, k == 0)
            split(0, 0, KT)
            split(1, 1, KT)

            pk = [prm[:, n * GP:(n + 1) * GP] for n in range(16)]
            a_re, a_im, dt = pk[0], pk[1], pk[2]
            tt, ts, stt = dve.tensor_tensor, dve.tensor_scalar, dve.scalar_tensor_tensor
            pv = pw[:].rearrange("p (l r k q) -> p l r k q", l=NL, r=2, k=2)
            m = prm[:, 9 * GP:11 * GP].rearrange("p (k q) -> p k q", k=2)
            m2 = prm[:, 11 * GP:13 * GP].rearrange("p (k q) -> p k q", k=2)

            def wide(ap, n):
                return ap.rearrange("p (q o) -> p q o", o=1).to_broadcast([P, GP, n])

            def cmul(out, a_r, a_i, src, n):
                s4 = src[:].rearrange("p (r q c) -> p r q c", r=2, q=GP)
                o4 = out[:].rearrange("p (r q c) -> p r q c", r=2, q=GP)
                t4 = btmp[:, 0:2 * GP * n].rearrange("p (r q c) -> p r q c", r=2, q=GP)
                tt(t4[:, 0], s4[:, 0], a_r, ALU.mult)
                after(tt(t4[:, 1], s4[:, 1], a_i, ALU.mult))
                after(tt(o4[:, 0], t4[:, 0], t4[:, 1], ALU.subtract))
                tt(t4[:, 0], s4[:, 1], a_r, ALU.mult)
                after(tt(t4[:, 1], s4[:, 0], a_i, ALU.mult))
                after(tt(o4[:, 1], t4[:, 0], t4[:, 1], ALU.add))

            def angles():
                dve.wait_ge(prm_in, 160)
                dve.wait_ge(sem("prm_act"), 1)
                tt(pk[3], a_re, dt, ALU.mult).then_inc(sem("prm_dve"), 1)
                after(tt(pk[4], a_im, dt, ALU.mult))
                after(ts(pk[5], pk[4], 1.0 / (2 * PI), MAGIC, ALU.mult, ALU.add))
                after(ts(pk[6], pk[4], 1.0 / (2 * PI), 0.25, ALU.mult, ALU.add))
                after(ts(pk[6], pk[6], MAGIC, None, ALU.add))
                after(ts(prm[:, 7 * GP:9 * GP], prm[:, 5 * GP:7 * GP], MAGIC, None, ALU.subtract))
                TURN = 6.28125
                for n in range(2):
                    after(stt(pk[5 + n], pk[7 + n], -TURN, pk[4], ALU.mult, ALU.add))
                    after(stt(pk[5 + n], pk[7 + n], -(2 * PI - TURN), pk[5 + n], ALU.mult, ALU.add))
                after(ts(pk[6], pk[6], PI / 2, None, ALU.add))
                ts(prm[:, 5 * GP:7 * GP], prm[:, 5 * GP:7 * GP], 3.1415925, -3.1415925, ALU.min,
                   ALU.max).then_inc(sem("prm_dve"), 1)

            def powers(levels):
                if levels[0] == 1:
                    dve.wait_ge(sem("prm_act"), 3)
                    tt(pv[:, 0, 0, 0], pk[3], pk[6], ALU.mult)
                    tt(pv[:, 0, 1, 0], pk[3], pk[5], ALU.mult)
                    dve.tensor_copy(pv[:, 0, 0, 1], pk[6])
                    after(dve.tensor_copy(pv[:, 0, 1, 1], pk[5]))
                for lev in levels:
                    re, im = pv[:, lev - 1, 0], pv[:, lev - 1, 1]
                    tt(m, re, re, ALU.mult)
                    tt(m2, im, im, ALU.mult)
                    after(stt(pv[:, lev, 1], re, 2.0, im, ALU.mult, ALU.mult))
                    after(tt(pv[:, lev, 0], m, m2, ALU.subtract))

            def factor():
                after(tt(mag8[:], pk[3], pk[3], ALU.mult))
                after(tt(mag8[:], mag8[:], mag8[:], ALU.mult))
                after(tt(mag8[:], mag8[:], mag8[:], ALU.mult))
                tt(pk[9], a_re, a_re, ALU.mult)
                after(tt(pk[10], a_im, a_im, ALU.mult))
                after(tt(pk[9], pk[9], pk[10], ALU.add))
                after(dve.reciprocal(pk[10], pk[9]))
                after(ts(pk[11], pv[:, 0, 0, 0], -1.0, None, ALU.add))
                tt(pk[12], pk[11], a_re, ALU.mult)
                after(tt(pk[13], pv[:, 0, 1, 0], a_im, ALU.mult))
                after(tt(pk[12], pk[12], pk[13], ALU.add))
                tt(pk[14], pv[:, 0, 1, 0], a_re, ALU.mult)
                after(tt(pk[15], pk[11], a_im, ALU.mult))
                after(tt(pk[13], pk[14], pk[15], ALU.subtract))
                after(tt(pk[12], pk[12], pk[10], ALU.mult))
                after(tt(pk[13], pk[13], pk[10], ALU.mult))

            def inputs():
                cmul(bb, wide(pk[12], GC), wide(pk[13], GC), braw, GC)

            def states():
                cmul(ah0, wide(pv[:, 0, 0, 0], NS), wide(pv[:, 0, 1, 0], NS), h0, NS)
                after(ts(cc[:, GP * GC:2 * GP * GC], cc[:, GP * GC:2 * GP * GC], -1.0, None, ALU.mult))
                dve.sem_inc(sem("bb_done"), 1)

            def prepare(it, b, u):
                if u == 2:
                    angles()
                elif u == 4:
                    powers(range(1, 5))
                elif u == 5:
                    powers(range(5, NL))
                elif u == 6:
                    factor()
                elif u == 7:
                    inputs()
                elif u == 8:
                    states()

            def qkv(it, b, u):
                dve.wait_ge(units_done, u + 3)
                dve.tensor_tensor(halves(tiles(qkvT, 2 * it + b)), acc(b), halves(rstd[:]),
                                  ALU.mult).then_inc(evac, 1)

            stage("qkv", qkv, prepare)
            dve.wait_ge(consts_in, 16 * 18)
            dve.tensor_scalar(nsink[:], sink[:], -1.0, None, ALU.mult)
            after(dve.tensor_scalar(nsink_row[:], sink_row[:], -1.0, None, ALU.mult))
            dve.wait_ge(sem("qk_sd"), 1)
            dve.reciprocal(qk_rms[0:2 * QK, :], qk_rms[0:2 * QK, :]).then_inc(sem("qk_rstd"), 1)
            for t in range(QK):
                dve.wait_ge(sem("qk_spread"), t + 1)
                g = 0 if t < 8 else 1
                stt(halves(tiles(qkvT, t)), halves(tiles(qkvT, t)), qk_gain[:, g:g + 1], misc[t % 2], ALU.mult,
                    ALU.mult).then_inc(sem("qk_normed"), 1)
            dve.wait_ge(sem("rows_turned"), 1)
            dve.tensor_copy(new_rows[0:NS, :], ps[0:NS, 2, :]).then_inc(sem("new_rows_done"), 1)
            dve.wait_ge(sem("qk_normed"), 10)
            dve.tensor_copy(ksT[:].rearrange("p (n k t) -> p n k t", n=NS, k=2)[:, :, :, P - 1:P],
                            tiles(qkvT, 8, 2).rearrange("p (k t o) -> p t k o", k=2, o=1)[:, SEQ:TOK]
                            ).then_inc(sem("ksT_new"), 1)
            def attn_max(a):
                b = a % 2
                dve.wait_ge(sem("scored"), a + 1)
                after(dve.tensor_reduce(soft[:, 16 * b:16 * b + 4],
                                        ps[:, 2 * b:2 * b + 2, :].rearrange("p b (m c) -> p b m c", m=2),
                                        AX.X, ALU.max))
                h = a_head(a)
                ts(soft[:, 16 * b + 4:16 * b + 8], soft[:, 16 * b:16 * b + 4], -SCALE, nsink[:, h:h + 1],
                   ALU.mult, ALU.min).then_inc(sem("maxed"), 1)

            def attn_norm(a):
                b = a % 2
                dve.wait_ge(sem("exp_done"), a + 1)
                s = soft[:, 16 * b:16 * b + 16]
                after(tt(s[:, 8:12], s[:, 8:12], s[:, 12:16], ALU.add))
                after(dve.reciprocal(s[:, 12:16], s[:, 8:12]))
                for blk in range(NB):
                    lo = P if blk == 0 else 0
                    v = probs[b][:, blk * 256 + lo:(blk + 1) * 256]
                    ins = ts(v, v, s[:, 12 + blk:13 + blk], None, ALU.mult)
                ins.then_inc(sem("p_done"), 1)

            attn_max(0)
            attn_max(1)
            dve.wait_ge(sem("s_turned"), 1)
            after(dve.tensor_reduce(s_soft[:, 0:1], ps[:, 6, 0:P], AX.X, ALU.max))
            ts(s_soft[:, 1:2], s_soft[:, 0:1], -SCALE, nsink_row[:], ALU.mult, ALU.min).then_inc(sem("s_maxed"), 1)
            dve.wait_ge(sem("s_exp"), 1)
            after(tt(s_soft[:, 4:5], s_soft[:, 2:3], s_soft[:, 3:4], ALU.add))
            after(dve.reciprocal(s_soft[:, 5:6], s_soft[:, 4:5]))
            ts(s_pr[:], s_pr[:], s_soft[:, 5:6], None, ALU.mult).then_inc(sem("s_pr_done"), 1)
            attn_norm(0)
            dve.wait_ge(sem("o_hi"), 1)
            sc = ps[:, 5, 0:NS * KT].rearrange("p (n k) -> p k n", n=NS)
            tt(op_lo[:].rearrange("p (k t) -> p k t", k=KT)[:, :, SEQ:TOK], sc,
               op_hi[:].bitcast(F32).rearrange("p (k t) -> p k t", k=KT)[:, :, SEQ:TOK],
               ALU.subtract).then_inc(op_ready, 1)

            def attn_turn(a):
                dve.wait_ge(sem("p_turned"), a + 1)
                if a >= 2:
                    dve.wait_ge(sem("pv_done"), a - 1)
                dve.tensor_copy(probsT[a % 2][:, 512:896], ps[:, 5, 0:384]).then_inc(sem("pT_dve"), 1)

            def attn_out(a):
                if a % 2:
                    j = a // 2
                    dve.wait_ge(sem("o_hi"), j + 2)
                    tt(tiles(op_lo, j)[:, 0:SEQ], ps[:, 6 + j % 2, :], tiles(op_hi, j)[:, 0:SEQ].bitcast(F32),
                       ALU.subtract).then_inc(op_ready, 1)

            for a in range(HEADS):
                attn_turn(a)
                if a + 1 < HEADS:
                    attn_norm(a + 1)
                if a + 2 < HEADS:
                    attn_max(a + 2)
                if a >= 1:
                    attn_out(a - 1)
            attn_out(HEADS - 1)

            def residual(name, n=None):
                def take(it, b, u):
                    m = 2 * it + b
                    dve.wait_ge(units_done, u + 3)
                    tt(halves(tiles(x, m)), acc(b), halves(tiles(x, m)), ALU.add).then_inc(evac, 1)

                def work(it, b, u):
                    if n is not None:
                        dve.wait_ge(evac, u + 3)
                        norm_in(n, 2 * it + b, b, isinstance(it, int) and it == 0 and b == 0)

                stage(name, take, work)

            def ffn(layer, half):
                hb = (2 * layer + half) * NPAIR
                if half == 0:
                    dve.wait_ge(sem("pre_done"), layer + 1)
                    if layer == 0:
                        dve.wait_ge(sem("attn_stored"), 1)
                    for b in range(2):
                        ins = dve.memset(up_row[b][:, 0:2], 0.0)
                    after(ins)

                def hid_lo_of(it):
                    dve.wait_ge(hid_hi_done, hb + it + 1)
                    dve.wait_ge(hid_prod, hb + it + 1)
                    tt(tiles(hid_lo, it), hid[:], tiles(hid_hi, it).bitcast(F32),
                       ALU.subtract).then_inc(hid_ready, 1)

                def take(it, b, u):
                    n = 2 * (hb + it) + b
                    dve.wait_ge(units_done, u + 3)
                    if not (hb == 0 and isinstance(it, int) and it == 0):
                        dve.wait_ge(conv_first, n - 1)
                        dve.wait_ge(conv_done, n - 1)
                    tt(halves(up_row[b][:, 2:UCOL]), acc(b), halves(rstd[:]), ALU.mult).then_inc(evac, 1)

                def work(it, b, u):
                    t = 2 * it + b + 22 * half
                    n = 2 * (hb + it) + b
                    dve.wait_ge(evac, u + 3)
                    dve.wait_ge(conv_first, n + 1)
                    c = conv[b]
                    stt(c[:, 0:SEQ], up_row[b][:, 0:SEQ], cw[:, bass.ds(t * 3, 1)], c[:, 0:SEQ],
                        ALU.mult, ALU.add).then_inc(conv_part, 1)
                    tt(c[:, SEQ:TOK], c[:, SEQ:TOK], pre[:, bass.ds(t * NS, NS)], ALU.add)
                    dve.wait_ge(conv_part, n + 1)
                    stt(c[:, 0:SEQ], up_row[b][:, 1:1 + SEQ], cw[:, bass.ds(t * 3 + 1, 1)], c[:, 0:SEQ],
                        ALU.mult, ALU.add).then_inc(conv_done, 1)
                    if b == 0:
                        if not isinstance(it, int) or it > 0:
                            hid_lo_of(it - 1)
                    else:
                        dve.wait_ge(silu_done, hb + it + 1)
                        dve.wait_ge(conv_done, n + 1)
                        if not (hb == 0 and isinstance(it, int) and it == 0):
                            dve.wait_ge(hid_ready, hb + it)
                        tt(hid[:], silu_g[:], c[:], ALU.mult).then_inc(hid_prod, 1)

                stage(f"up{layer}{half}", take, work)
                hid_lo_of(NPAIR - 1)
                residual(f"dn{layer}{half}", 2 if (layer, half) == (0, 1) else None)

            residual("wo", 1)
            ffn(0, 0)
            ffn(0, 1)

            tt(skip_d[:].rearrange("p (g c) -> p g c", c=GC),
               dskip[:].rearrange("p (g o) -> p g o", o=1).to_broadcast([P, GROUPS, GC]),
               ident[:, P - GC:P].rearrange("p (o c) -> p o c", o=1).to_broadcast([P, GROUPS, GC]),
               ALU.mult).then_inc(sem("skip_made"), 1)
            sel = rstd_u[:, NS:NS + NC]
            per_step = rstd[:, 0:SEQ].rearrange("p (c s) -> p s c", s=CH)
            u3 = u_in[:].rearrange("p (g c) -> p g c", g=GROUPS)

            def scale_u(k):
                v = u3[:, CH * k:CH * (k + 1), :]
                tt(v, v, rstd_u[:].rearrange("p (o c) -> p o c", o=1).to_broadcast([P, CH, UW]),
                   ALU.mult).then_inc(sem("u_ready"), 1)

            for j in range(NJ):
                dve.wait_ge(sem("resp_done"), j + 1)
                dve.tensor_copy(wst[:, j * 1024 + 512:(j + 1) * 1024],
                                ps[:, 2 * (j % 2) + 1, :]).then_inc(sem("wst_dve"), 1)
                if j < 4:
                    dve.wait_ge(sd_done, 3)
                    q = slice(j * TOK // 4, (j + 1) * TOK // 4)
                    ins = dve.reciprocal(rstd[:, q], sq[0][:, q])
                    if j == 3:
                        ins.then_inc(rstd_done, 1)
                        dve.wait_ge(rstd_done, 3)
                if j == 4:
                    dve.tensor_copy(rstd_u[:, 0:NS], rstd[:, SEQ:TOK])
                    dve.tensor_copy(rstd_u[:, NS + NC:UW], rstd[:, SEQ:TOK])
                    after(ts(sel, per_step[:, 0], step_sel[:, 0:1], None, ALU.mult))
                    for s in range(1, CH):
                        after(stt(sel, per_step[:, s], step_sel[:, s:s + 1], sel, ALU.mult, ALU.add))
                if j >= 5:
                    dve.wait_ge(sem("u_in"), 16 * (CH + 2) * KT)
                    scale_u(j - 5)
                if j % 4 == 3:
                    h = j // 4
                    dve.wait_ge(sem("rsb_done"), h + 1)
                    dve.wait_ge(sem("skip_made"), 1)
                    tt(rsb[h][:, 0:512], rsb[h][:, 0:512], skip_d[:, h * 512:(h + 1) * 512],
                       ALU.add).then_inc(sem("rsb_full"), 1)
            dve.wait_ge(sem("rsb_full"), 2)
            for k in range(3, KT):
                scale_u(k)

            def z_part(j):
                dve.wait_ge(sem("z_hi"), j + 1)
                dve.wait_ge(sem("x_fin_done"), j + 1)
                c0 = j * TOK
                in_steps = "p (c b s) -> p b s c"
                tt(z_lo[:, c0:c0 + SEQ].rearrange(in_steps, b=2, s=CH // 2), turned,
                   z_hi[:, c0:c0 + SEQ].bitcast(F32).rearrange(in_steps, b=2, s=CH // 2), ALU.subtract)
                tt(z_lo[:, c0 + SEQ:c0 + TOK], ps[:, 6, 0:NS],
                   z_hi[:, c0 + SEQ:c0 + TOK].bitcast(F32), ALU.subtract).then_inc(op_ready, 1)

            a4 = ah0[:].rearrange("p (r q n) -> p r q n", r=2, q=GP)
            for j in range(NJ):
                b = j % 2
                v = [ps[:, 2 * b + ri, 0:288].rearrange("p (q c) -> p q c", q=JQ) for ri in range(2)]
                e = rots[b][:].rearrange("p (r q c) -> p r q c", r=2, q=JQ)
                vr = [t[:].rearrange("p (q c) -> p q c", q=JQ) for t in vrot]
                vt = [t[:].rearrange("p (q c) -> p q c", q=JQ) for t in vtmp]
                dve.wait_ge(sem("v_done"), j + 1)
                dve.wait_ge(sem(f"e_in{b}"), 16 * (j // 2 + 1))
                tt(vt[0], v[0][:, :, 0:NC], e[:, 0], ALU.mult)
                after(tt(vt[1], v[1][:, :, 0:NC], e[:, 1], ALU.mult))
                after(tt(vr[0], vt[0], vt[1], ALU.add))
                tt(vt[0], v[1][:, :, 0:NC], e[:, 0], ALU.mult)
                after(tt(vt[1], v[0][:, :, 0:NC], e[:, 1], ALU.mult))
                after(tt(vr[1], vt[0], vt[1], ALU.subtract))
                for ri in range(2):
                    ins = tt(a4[:, ri, JQ * j:JQ * (j + 1), :], v[ri][:, :, NC:NC + NS],
                             a4[:, ri, JQ * j:JQ * (j + 1), :], ALU.add)
                ins.then_inc(sem("v_used"), 1)
                if j >= 2:
                    dve.wait_ge(sem("x_done"), j - 1)
                for ri in range(2):
                    for q in range(JQ):
                        at = (ri * JQ + q) * NC
                        ins = dve.tensor_tensor_scan(
                            zst[b][:, at:at + NC],
                            mag8[:, JQ * j + q:JQ * j + q + 1].to_broadcast([P, NC]),
                            vrot[ri][:, q * NC:(q + 1) * NC], 0.0, ALU.mult, ALU.add)
                ins.then_inc(sem("z_done"), 1)
                dve.wait_ge(sem("z_done"), j + 1)
                if j >= 3:
                    z_part(j - 3)
            for j in range(NJ - 3, NJ):
                z_part(j)

            def glu(it, b, u):
                dve.wait_ge(units_done, u + 3)
                if b == 0:
                    dve.tensor_copy(halves(glu_in[0][:]), acc(0)).then_inc(evac, 1)
                    dve.wait_ge(evac, u + 3)
                else:
                    dve.wait_ge(sem("tanh_done"), it + 1)
                    stt(glu_out[:], glu_in[1][:], 1.0, glu_in[0][:], ALU.add, ALU.mult).then_inc(evac, 1)
                    dve.wait_ge(evac, u + 3)
                    stt(tiles(x, it), glu_out[:], 0.5, tiles(x, it), ALU.mult, ALU.add).then_inc(sem("glu_done"), 1)
                    dve.wait_ge(sem("glu_done"), it + 1)
                    norm_in(3, it, 0, isinstance(it, int) and it == 0)

            stage("glu", None, glu)
            ffn(1, 0)
            ffn(1, 1)

        @block.tensor
        def _(pe):
            def unit(stage, n, b, hi, lo, kwait=None):
                kt = INFO[stage][4]
                u = BASE[stage] + 2 * n + b
                pe.wait_ge(lo_done, u + 3)
                pe.wait_ge(evac, u + 1)
                for k in range(kt):
                    if kwait:
                        pe.wait_ge(kwait[0], kwait[1] + k + 1)
                    wh, wl = w_hi[b][:, k * P:(k + 1) * P], w_lo[b][:, k * P:(k + 1) * P]
                    for h in range(2):
                        c0 = k * TOK + h * HALF
                        xh, xl = hi[:, c0:c0 + HALF], lo[:, c0:c0 + HALF]
                        out = ps[:, 2 * b + h, 0:HALF]
                        pe.matmul(out, wh, xh, start=(k == 0), stop=False)
                        pe.matmul(out, wh, xl, start=False, stop=False)
                        ins = pe.matmul(out, wl, xh, start=False, stop=(k == kt - 1))
                ins.then_inc(units_done, 1)

            def norm_stat(n):
                pe.wait_ge(sqs_done, KT * (n + 1))
                for h in range(2):
                    ins = pe.matmul(misc[0][:, h], ones[:], sqs[:, h * HALF:(h + 1) * HALF],
                                    start=True, stop=True)
                ins.then_inc(stat_done, 1)

            def stage(name, hi, lo, ready):
                if name == "qkv":
                    norm_stat(0)
                unit(name, 0, 0, hi, lo, ready)
                if name in NORM_OF and name != "qkv":
                    norm_stat(NORM_OF[name])
                unit(name, 0, 1, hi, lo)
                with pe.Fori(1, INFO[name][3] // 2) as n:
                    for b in range(2):
                        unit(name, n, b, hi, lo)

            pe.sem_inc(units_done, 2)
            pe.wait_ge(consts_in, 16 * 18)
            stage("qkv", hx_hi, hx_lo, (hx_ready, 0))

            pe.wait_ge(sd_done, 1)
            for t in range(QK):
                pe.wait_ge(sem("qk_sq"), t + 1)
                for h in range(2):
                    ins = pe.matmul(ps[0:2 * QK, 4 + h, 0:HALF],
                                    head_mean[:, 2 * (QK - 1 - t):2 * (QK - 1 - t) + 2 * QK],
                                    sq[t % 2][:, h * HALF:(h + 1) * HALF], start=(t == 0), stop=(t == QK - 1))
                ins.then_inc(sem("qk_summed"), 1)

            def spread(t):
                pe.wait_ge(sem("qk_rstd"), 1)
                if t >= 2:
                    pe.wait_ge(sem("qk_normed"), t - 1)
                for h in range(2):
                    ins = pe.matmul(misc[t % 2][:, h], head_rows[0:2 * QK, t * P:(t + 1) * P],
                                    qk_rms[0:2 * QK, h * HALF:(h + 1) * HALF], start=True, stop=True)
                ins.then_inc(sem("qk_spread"), 1)

            def qt(t, c0, n, e=None):
                rows = slice(0, P) if e is None else slice(64 * e, 64 * e + 64)
                return qkvT[rows, t * TOK + c0:t * TOK + c0 + n]

            pe.wait_ge(evac, BASE["wo"] + 2)
            for blk in range(NB):
                for v in range(2):
                    ins = pe.transpose(ps[:, blk // 2, (blk % 2) * 256 + v * P:(blk % 2) * 256 + (v + 1) * P],
                                       qt(10 + v, blk * P, P), ident[:])
            ins.then_inc(sem("v_turned"), 1)
            for t in range(QK):
                spread(t)
            pe.wait_ge(sem("qk_normed"), 10)
            for v in range(4):
                ins = pe.transpose(ps[0:NS, 2, v * P:(v + 1) * P], qt((10, 11, 8, 9)[v], SEQ, NS), ident[:])
            ins.then_inc(sem("rows_turned"), 1)
            pe.wait_ge(sem("kc_in"), 16)
            for n in range(NS):
                for p in range(2):
                    m = 2 * n + p
                    ins = pe.transpose(ps[:, 4 + m // 4, (m % 4) * P:(m % 4) * P + P - 1],
                                       kc[0:P - 1, n * 256 + p * P:n * 256 + (p + 1) * P],
                                       ident[0:P - 1, 0:P - 1])
            ins.then_inc(sem("ks_turned"), 1)
            def scores(a):
                b, (p, g, e) = a % 2, a_split(a)
                if a >= 2:
                    pe.wait_ge(sem("exp_done"), a - 1)
                elif a == 0:
                    pe.wait_ge(sem("vtok_done"), 1)
                else:
                    pe.wait_ge(sem("new_rows_done"), 1)
                r = slice(64 * e, 64 * e + 64)
                for bank in range(2):
                    pe.matmul(ps[:, 2 * b + bank, :], ident16[:], masks[:, bank * 512:(bank + 1) * 512],
                              start=True, stop=False, skip_group_check=True)
                    for blk in (2 * bank, 2 * bank + 1):
                        k0 = max(blk - 1, 0)
                        w = (blk - k0 + 1) * P
                        c1 = (blk % 2) * 256 + 256
                        ins = pe.matmul(ps[:, 2 * b + bank, c1 - w:c1],
                                        qkvT[r, (4 * p + g) * TOK + blk * P:(4 * p + g) * TOK + (blk + 1) * P],
                                        qkvT[r, (8 + p) * TOK + k0 * P:(8 + p) * TOK + k0 * P + w],
                                        start=False, stop=(blk % 2 == 1), skip_group_check=True)
                ins.then_inc(sem("scored"), 1)

            pe.wait_ge(sem("new_rows_done"), 1)
            pe.wait_ge(sem("ksT_done"), 1)
            pe.wait_ge(sem("ksT_new"), 1)
            q3 = qkvT[:].rearrange("p (t c) -> p t c", t=12)
            for n in range(NS):
                for p in range(2):
                    for e in range(2):
                        r = slice(64 * e, 64 * e + 64)
                        c0 = n * 8 + p * 4
                        ins = pe.matmul(ps[:, 4 + e, c0:c0 + 4], ksT[r, (2 * n + p) * P:(2 * n + p + 1) * P],
                                        q3[r, 4 * p:4 * p + 4, SEQ + n], start=True, stop=True)
            ins.then_inc(sem("s_scored"), 1)
            scores(0)
            scores(1)
            pe.wait_ge(sem("s_st_done"), 1)
            pe.wait_ge(sem("vtok_done"), 1)
            pe.transpose(ps[:, 6, 0:P], s_st[:], ident[:]).then_inc(sem("s_turned"), 1)
            pe.wait_ge(sem("s_pr_done"), 1)
            pe.transpose(ps[:, 7, 0:P], s_pr[:], ident[:]).then_inc(sem("s_pturned"), 1)
            pe.wait_ge(sem("s_pT_done"), 1)
            pe.wait_ge(sem("vc_new"), 16 * NS)
            pe.wait_ge(cache_in, 16)
            pe.wait_ge(sem("new_rows_done"), 1)
            for n in range(NS):
                for p in range(2):
                    for e in range(2):
                        c0 = n * HEADS + p * 8 + e * 4
                        kv = 2 * p + e
                        ins = pe.matmul(ps[64 * e:64 * e + 64, 5, n * KT + 4 * p:n * KT + 4 * p + 4],
                                        vc[:, n * 256 + kv * HD:n * 256 + (kv + 1) * HD],
                                        s_pT[:, c0:c0 + 4], start=True, stop=True)
            ins.then_inc(sem("s_out"), 1)

            def turn(a):
                b = a % 2
                pe.wait_ge(sem("p_done"), a + 1)
                if a >= 1:
                    pe.wait_ge(sem("pT_act"), a)
                    pe.wait_ge(sem("pT_dve"), a)
                else:
                    pe.wait_ge(op_ready, 1)
                for blk in range(NB):
                    for prev in ((0,) if blk == 0 else (1, 0)):
                        slot = 2 * blk - prev
                        c0 = blk * 256 + (0 if prev else P)
                        ins = pe.transpose(ps[:, 4 + slot // 4, (slot % 4) * P:(slot % 4) * P + P],
                                           probs[b][:, c0:c0 + P], ident[:])
                ins.then_inc(sem("p_turned"), 1)

            def pv(a):
                b, (p, g, e) = a % 2, a_split(a)
                pe.wait_ge(sem("pT_act"), a + 1)
                pe.wait_ge(sem("pT_dve"), a + 1)
                j = a // 2
                if e == 0 and j >= 2:
                    pe.wait_ge(op_ready, j)
                kv = 2 * p + e
                for blk in range(NB):
                    for prev in ((0,) if blk == 0 else (1, 0)):
                        slot = 2 * blk - prev
                        ins = pe.matmul(ps[64 * e:64 * e + 64, 6 + j % 2, blk * P:(blk + 1) * P],
                                        vtok[:, (blk - prev) * 256 + kv * HD:(blk - prev) * 256 + (kv + 1) * HD],
                                        probsT[b][:, slot * P:(slot + 1) * P],
                                        start=(prev == 1 or blk == 0), stop=(prev == 0))
                ins.then_inc(sem("pv_done"), 1)

            for a in range(HEADS):
                turn(a)
                if a + 2 < HEADS:
                    scores(a + 2)
                pv(a)

            pe.wait_ge(op_ready, 9)
            stage("wo", op_hi, op_lo, (op_ready, 1))
            stage("up00", hx_hi, hx_lo, (hx_ready, KT))
            stage("dn00", hid_hi, hid_lo, (hid_ready, 0))
            stage("up01", hx_hi, hx_lo, None)
            stage("dn01", hid_hi, hid_lo, (hid_ready, NPAIR))

            norm_stat(2)
            pe.wait_ge(evac, BASE["glu"] + 2)
            for j in range(NJ):
                g4 = wst[:, j * 1024:(j + 1) * 1024].rearrange("p (q r n) -> p q r n", q=JQ, r=2)
                if j == 0:
                    pe.wait_ge(sem("g_in"), 16 * NJ)
                pe.wait_ge(sem("ccd_done"), j + 1)
                if j >= 2:
                    pe.wait_ge(sem("wst_act"), j - 1)
                    pe.wait_ge(sem("wst_dve"), j - 1)
                for q in range(JQ):
                    gp = JQ * j + q
                    c0 = (gp % 16) * 2 * GC
                    for ri in range(2):
                        pe.matmul(ps[:, 6 + gp // 16, c0:c0 + 2 * GC], g4[:, q, ri, :],
                                  ccd_view(j)[:, q, ri], start=(ri == 0), stop=(ri == 1))
                    for ri in range(2):
                        m = 2 * q + ri
                        ins = pe.transpose(ps[:, 2 * (j % 2) + m // 4, (m % 4) * P:(m % 4) * P + P],
                                           g4[:, q, ri, :], ident[:])
                ins.then_inc(sem("resp_done"), 1)

            def states_in(j):
                pe.wait_ge(sem("u_ready"), j + 1)
                if j >= 2:
                    pe.wait_ge(sem("v_used"), j - 1)
                for q in range(JQ):
                    gp = JQ * j + q
                    for ri in range(2):
                        for e in range(2):
                            g = 2 * gp + e
                            c0 = (gp * 2 + ri) * P + 64 * e
                            ins = pe.matmul(ps[64 * e:64 * e + 64, 2 * (j % 2) + ri, q * 72:(q + 1) * 72],
                                            wst[:, c0:c0 + 64], u_in[:, g * UW + NS:(g + 1) * UW],
                                            start=True, stop=True)
                ins.then_inc(sem("v_done"), 1)

            def outputs(j):
                pe.wait_ge(sem(f"c_in{j % 2}"), 16 * (j // 2 + 1))
                pe.wait_ge(sem("x_done"), j + 1)
                if j == 0:
                    pe.wait_ge(sem("toep_in0"), 16 * CH)
                    pe.wait_ge(sem("x_seeded"), 1)
                    pe.wait_ge(sem("rsb_done"), 2)
                if j == NJ // 2:
                    pe.wait_ge(sem("toep_in1"), 16 * CH)
                if j >= 1:
                    pe.wait_ge(sem("yc_done"), j)
                c5 = recs[j % 2][:].rearrange("p (q r n) -> p q r n", q=JQ, r=2)
                t3 = toep[:].rearrange("p (h t g c) -> p h t g c", h=2, t=CH, c=GC)
                for q in range(JQ):
                    gp = JQ * j + q
                    for e in range(2):
                        r = slice(64 * e, 64 * e + 64)
                        g = 2 * gp + e
                        out = ps[0:YW, 4 + e, q * P:(q + 1) * P]
                        pe.matmul(out, u_in[:, g * UW:g * UW + YW], t3[:, g // 32, :, g % 32, :],
                                  start=True, stop=False)
                        for ri in range(2):
                            c0 = (gp * 2 + ri) * XW
                            ins = pe.matmul(out, xst[r, c0:c0 + YW], c5[r, q, ri, :], start=False,
                                            stop=(ri == 1))
                ins.then_inc(sem("y_mm"), 1)

            def turn_outputs(j):
                pe.wait_ge(sem("yc_done"), j + 1)
                if j >= 1:
                    pe.wait_ge(op_ready, 9 + j)
                for t in range(CH):
                    ins = pe.transpose(ps[:, 6 + t // 4, (t % 4) * YW:(t % 4 + 1) * YW],
                                       yc[j % 2][0:YW, t * P:(t + 1) * P], ident[0:YW, 0:YW])
                ins.then_inc(sem("z_turned"), 1)

            pe.wait_ge(sem("wst_act"), NJ)
            pe.wait_ge(sem("wst_dve"), NJ)
            for j in range(NJ + 3):
                if j < NJ:
                    states_in(j)
                if j >= 3:
                    turn_outputs(j - 3)
                if 2 <= j < NJ + 2:
                    outputs(j - 2)

            stage("glu", z_hi, z_lo, (op_ready, 9))
            stage("up10", hx_hi, hx_lo, (hx_ready, 2 * KT))
            stage("dn10", hid_hi, hid_lo, (hid_ready, 2 * NPAIR))
            stage("up11", hx_hi, hx_lo, None)
            stage("dn11", hid_hi, hid_lo, (hid_ready, 3 * NPAIR))


def kernel(**inputs):
    import numpy as np
    import concourse.bacc as _bacc
    from concourse import mybir as _mybir
    from concourse.bass_utils import run_bass_kernel_spmd as _run

    a = {k: np.asarray(v) for k, v in inputs.items()}
    f = a["x_prompt"].dtype
    d = {}
    d["xT"] = np.concatenate([a["x_prompt"].reshape(SEQ, D), a["x_sample"].reshape(NS, D)]).T
    wq = a["w_qkv"][0]
    q = wq[:, :D].reshape(KT, P, 2, 2, 4, HD).transpose(2, 4, 1, 0, 3, 5).reshape(8, P, KT * P)
    kv = wq[:, D:].reshape(KT, P, 4, P).transpose(2, 1, 0, 3).reshape(4, P, KT * P)
    d["wqkv"] = np.concatenate([q, kv])
    d["wo"] = a["w_o"][0].reshape(2, 2, 4, HD, KT, P).transpose(4, 1, 3, 0, 2, 5).reshape(KT, P, KT * P)
    d["wglu"] = a["w_glu"][0].reshape(KT, P, 2, KT, P).transpose(3, 2, 1, 0, 4).reshape(2 * KT, P, KT * P)
    d["wup"] = a["w_up"].reshape(2, KT, P, 2, 2 * NPAIR, P).transpose(0, 4, 3, 2, 1, 5).reshape(-1, P, KT * P)
    d["wdn"] = a["w_down"].reshape(2, 2, NPAIR, P, KT, P).transpose(0, 1, 4, 3, 2, 5).reshape(-1, P, NPAIR * P)
    d["ones"] = np.full((P, P), 1.0 / D, f)
    d["head_mean"] = np.zeros((P, 4 * QK - 2), f)
    for e in range(2):
        d["head_mean"][e * HD:(e + 1) * HD, 2 * QK - 2 + e] = 1.0 / HD
    d["head_rows"] = np.kron(np.eye(2 * QK), np.ones((1, HD))).astype(f)
    d["ident"] = np.eye(P, dtype=f)
    b16 = _mybir.dt.np(_mybir.dt.bfloat16)
    d["ident16"] = np.eye(P).astype(b16)
    r, c = np.arange(P)[:, None], np.arange(P)[None, :]
    off = np.full((P, P), -1e30)
    prev, same = np.where(c > r, 0.0, off), np.where(c <= r, 0.0, off)
    d["masks"] = np.concatenate([off, same, prev, same, prev, same, prev, same], 1).astype(b16)
    g = np.stack([a["norm_mix"][0], a["norm_ffn"][0], a["norm_mix"][1], a["norm_ffn"][1]])
    d["gains"] = g.reshape(4, KT, P).transpose(2, 0, 1).reshape(P, 4 * KT)
    d["qk_gain"] = np.concatenate([np.stack([a["q_norm"][0], a["k_norm"][0]], 1)] * 2)
    d["dskip"] = np.tile(a["ssm_d"][0].reshape(GROUPS, GC).T, (CH, 1))
    d["step_sel"] = np.kron(np.eye(CH), np.ones((GC, 1))).astype(f)
    d["sinks"] = a["sinks"]
    d["sink_col"] = a["sinks"].reshape(HEADS, 1)
    d["cache_k"] = a["cache_k"][0].reshape(NS, P, KVH * HD)
    d["cache_v"] = a["cache_v"][0].reshape(NS, P, KVH * HD)
    d["a_re"] = a["ssm_a_re"][0].reshape(GP, P).T
    d["a_im"] = a["ssm_a_im"][0].reshape(GP, P).T
    d["log_dt"] = a["ssm_log_dt"][0].reshape(GP, 2).T
    for n in ("re", "im"):
        d["b_" + n] = a["ssm_b_" + n][0].reshape(GP, P, GC).transpose(1, 0, 2).reshape(P, GP * GC)
        d["c_" + n] = a["ssm_c_" + n][0].reshape(GP, 2, GC, ST).transpose(1, 3, 0, 2).reshape(P, GP * GC)
        d["h0_" + n] = a["state_ssm_" + n][0].reshape(NS, GP, P).transpose(2, 1, 0).reshape(P, GP * NS)
    d["conv_w"] = a["conv_w"].reshape(2, 3, 2, 22, P).transpose(0, 4, 3, 2, 1).reshape(2, P, 132)
    d["conv_b"] = a["conv_b"].reshape(2, 2, 22, P).transpose(0, 3, 2, 1).reshape(2, P, 44)
    d["conv_buf"] = a["state_conv"].reshape(2, NS, 2, 2, 22, P).transpose(0, 5, 2, 4, 3, 1).reshape(2, P, -1)
    outs = {"yT": (D, TOK), "k_prompt": (P, 2, P), "v_prompt": (P, 2, P), "k_sample": (NS, P, KVH * HD),
            "v_sample": (NS, P, KVH * HD), "x_fin": (P, 2 * GP), "xs_new": (P, 2 * GP * NS),
            "conv_rows": (2, P, 440), "conv_second": (2, P, 44 * NS)}

    nc = _bacc.Bacc("TRN2", target_bir_lowering=False, num_devices=1)
    arrays, ins, res = {}, {}, {}
    for name, v in d.items():
        v = np.ascontiguousarray(v)
        arrays[f"in_{name}"] = v
        ins[name] = nc.dram_tensor(f"in_{name}", v.shape, _mybir.dt.from_np(v.dtype), kind="ExternalInput").ap()
    for name, shape in outs.items():
        res[name] = nc.dram_tensor(f"out_{name}", shape, _mybir.dt.from_np(f), kind="ExternalOutput").ap()
    trunk_program(nc, ins, res)
    got = _run(nc, [arrays], core_ids=[0]).results[0]
    o = {name: np.asarray(got[f"out_{name}"]) for name in outs}

    y = np.ascontiguousarray(o["yT"].T)
    rows = lambda t: np.ascontiguousarray(t.transpose(2, 1, 0)).reshape(1, 1, P, KVH, HD)
    cache = lambda t: t.reshape(1, NS, P, KVH, HD)
    fin = o["x_fin"].reshape(2, ST, GP, 2).transpose(3, 2, 0, 1).reshape(2, 1, 1, GROUPS, ST)
    new = o["xs_new"].reshape(2, ST, 2, GP, NS).transpose(2, 4, 3, 0, 1).reshape(2, 1, NS, GROUPS, ST)
    cr = o["conv_rows"].reshape(2, P, 22, 2, 10).transpose(0, 4, 3, 2, 1).reshape(2, 10, F2)
    cs = o["conv_second"].reshape(2, P, 22, 2, NS).transpose(0, 4, 3, 2, 1).reshape(2, NS, F2)
    con = np.ascontiguousarray
    return (y[:SEQ].reshape(1, SEQ, D), y[SEQ:].reshape(NS, 1, D), rows(o["k_prompt"]), rows(o["v_prompt"]),
            cache(o["k_sample"]), cache(o["v_sample"]), con(fin[0]), con(fin[1]), con(new[0]), con(new[1]),
            con(cr[:, None, :2]), con(np.stack([cs, cr[:, 2:]], 2)))
```
